# Optimizing a Trainium2 kernel written in Bass

```python
import jax, jax.numpy as jnp
from jax import lax
import numpy as np

D_MODEL = 1024
BATCH = 1
SEQ = 512
DEPTH = 2

GRID_W = 64
CTX_LEN = 256
Q_BLOCK = 128
ROPE_BASE = 10000.0
EPS = 1e-6
NEG_INF = -1e30

MLA_HEADS = 8
MLA_Q_RANK = 256
MLA_KV_RANK = 128
MLA_NOPE = 64
MLA_ROPE = 32
MLA_V = 64
SWA_HEADS = 8
SWA_KV_HEADS = 2
SWA_DIM = 64
SWA_WINDOW = 128
NA_HEADS = 8
NA_DIM = 64
NA_KH = 8
NA_KW = 16
GQA_HEADS = 4
GQA_KV_HEADS = 2
GQA_DIM = 128
D_FF = 2816
CONV_W = 3

EVEN_MLA_IN = MLA_Q_RANK + MLA_KV_RANK + MLA_ROPE
EVEN_SWA_IN = (SWA_HEADS + 2 * SWA_KV_HEADS) * SWA_DIM
EVEN_IN = EVEN_MLA_IN + EVEN_SWA_IN
EVEN_MIX = MLA_HEADS * MLA_V + SWA_HEADS * SWA_DIM
ODD_NA_IN = 3 * NA_HEADS * NA_DIM
ODD_GQA_IN = (GQA_HEADS + 2 * GQA_KV_HEADS) * GQA_DIM
ODD_IN = ODD_NA_IN + ODD_GQA_IN
ODD_MIX = NA_HEADS * NA_DIM + GQA_HEADS * GQA_DIM

kernel_name = 'hybrid_mla_swa_natten_gqa_convffn_prefix'

def rms_norm(x, g):
    xf = x.astype(jnp.float32)
    y = xf * lax.rsqrt(jnp.mean(xf * xf, axis=-1, keepdims=True) + EPS)
    return (y * g.astype(jnp.float32)).astype(x.dtype)

def modulate(x, g, shift, scale):
    return rms_norm(x, g) * (1 + scale) + shift

def rope_tables(n, d):
    t = jnp.arange(n)
    rows = (t // GRID_W).astype(jnp.float32)
    cols = (t % GRID_W).astype(jnp.float32)
    freqs = ROPE_BASE ** (-jnp.arange(d // 4, dtype=jnp.float32) * 4.0 / d)
    ang = jnp.concatenate([rows[:, None] * freqs, cols[:, None] * freqs], axis=-1)
    return jnp.cos(ang), jnp.sin(ang)

def apply_rope(x, cos, sin):
    h = x.shape[-1] // 2
    x1, x2 = x[..., :h], x[..., h:]
    cos = cos.astype(x.dtype)
    sin = sin.astype(x.dtype)
    return jnp.concatenate([x1 * cos - x2 * sin, x2 * cos + x1 * sin], axis=-1)

def heads(p, n_heads):
    b, n, _ = p.shape
    return p.reshape(b, n, n_heads, -1).transpose(0, 2, 1, 3)

def merge_heads(o):
    b, h, n, d = o.shape
    return o.transpose(0, 2, 1, 3).reshape(b, n, h * d)

def group_heads(q, n_kv):
    b, h, n, d = q.shape
    return q.reshape(b, n_kv, h // n_kv, n, d)

def split_qkv(p, nq_heads, nkv_heads, d):
    nq, nk = nq_heads * d, nkv_heads * d
    return (heads(p[..., :nq], nq_heads), heads(p[..., nq:nq + nk], nkv_heads),
            heads(p[..., nq + nk:], nkv_heads))

def softmax_with_sink(s, sink):
    sk = jnp.broadcast_to(sink.astype(jnp.float32)[None, :, :, None, None], s.shape[:-1] + (1,))
    return jax.nn.softmax(jnp.concatenate([s, sk], axis=-1), axis=-1)[..., :-1]

def dense_ctx_attention(q, kc, vc, scale, sink=None):
    s = jnp.einsum('bgrqd,bgkd->bgrqk', q, kc).astype(jnp.float32) * scale
    p = jax.nn.softmax(s, axis=-1) if sink is None else softmax_with_sink(s, sink)
    o = jnp.einsum('bgrqk,bgkd->bgrqd', p.astype(vc.dtype), vc)
    b, g, r, n, dv = o.shape
    return o.reshape(b, g * r, n, dv)

def blocked_global_attention(q, k, v, kc, vc, scale):
    b, g, r, s, d = q.shape
    nb = s // Q_BLOCK
    k_all = jnp.concatenate([kc, k], axis=2)
    v_all = jnp.concatenate([vc, v], axis=2)
    qb = q.reshape(b, g, r, nb, Q_BLOCK, d).transpose(3, 0, 1, 2, 4, 5)

    def block(qi):
        sc = jnp.einsum('bgrqd,bgkd->bgrqk', qi, k_all).astype(jnp.float32) * scale
        p = jax.nn.softmax(sc, axis=-1).astype(v_all.dtype)
        return jnp.einsum('bgrqk,bgkd->bgrqd', p, v_all)

    o = lax.map(block, qb)
    return o.transpose(1, 2, 3, 0, 4, 5).reshape(b, g * r, s, -1)

def banded_window_attention(q, k, v, kc, vc, sink, scale):
    b, g, r, s, d = q.shape
    nb = s // Q_BLOCK
    band = Q_BLOCK + 2 * SWA_WINDOW
    n_ctx = kc.shape[2]
    kp = jnp.pad(k, ((0, 0), (0, 0), (SWA_WINDOW, SWA_WINDOW), (0, 0)))
    vp = jnp.pad(v, ((0, 0), (0, 0), (SWA_WINDOW, SWA_WINDOW), (0, 0)))
    rel = jnp.arange(band)[None, :] - SWA_WINDOW - jnp.arange(Q_BLOCK)[:, None]
    in_window = jnp.abs(rel) <= SWA_WINDOW
    qb = q.reshape(b, g, r, nb, Q_BLOCK, d).transpose(3, 0, 1, 2, 4, 5)

    def block(args):
        qi, n = args
        start = n * Q_BLOCK
        kb = lax.dynamic_slice_in_dim(kp, start, band, axis=2)
        vb = lax.dynamic_slice_in_dim(vp, start, band, axis=2)
        kpos = start - SWA_WINDOW + jnp.arange(band)
        mask = in_window & ((kpos >= 0) & (kpos < s))[None, :]
        s_loc = jnp.einsum('bgrqd,bgkd->bgrqk', qi, kb).astype(jnp.float32) * scale
        s_loc = jnp.where(mask, s_loc, NEG_INF)
        s_ctx = jnp.einsum('bgrqd,bgkd->bgrqk', qi, kc).astype(jnp.float32) * scale
        p = softmax_with_sink(jnp.concatenate([s_ctx, s_loc], axis=-1), sink).astype(vb.dtype)
        return (jnp.einsum('bgrqk,bgkd->bgrqd', p[..., :n_ctx], vc)
                + jnp.einsum('bgrqk,bgkd->bgrqd', p[..., n_ctx:], vb))

    o = lax.map(block, (qb, jnp.arange(nb)))
    return o.transpose(1, 2, 3, 0, 4, 5).reshape(b, g * r, s, -1)

def mla_mixer(p_lat, p_ctx, q_norm_g, w_uq, kv_norm_g, w_ukv, need_ctx):
    def project(p):
        cq = p[..., :MLA_Q_RANK]
        ckv = p[..., MLA_Q_RANK:MLA_Q_RANK + MLA_KV_RANK]
        k_pe = p[..., MLA_Q_RANK + MLA_KV_RANK:]
        q = heads(rms_norm(cq, q_norm_g) @ w_uq, MLA_HEADS)
        kv = heads(rms_norm(ckv, kv_norm_g) @ w_ukv, MLA_HEADS)
        return q[..., :MLA_NOPE], q[..., MLA_NOPE:], kv[..., :MLA_NOPE], kv[..., MLA_NOPE:], k_pe[:, None]

    def assemble(q_nope, q_pe, k_nope, k_pe):
        q = jnp.concatenate([q_nope, q_pe], axis=-1)
        k = jnp.concatenate([k_nope, jnp.broadcast_to(k_pe, k_nope.shape[:-1] + (MLA_ROPE,))], axis=-1)
        return q[:, :, None], k

    q_nope, q_pe, k_nope, v, k_pe = project(p_lat)
    cos, sin = rope_tables(p_lat.shape[1], MLA_ROPE)
    q, k = assemble(q_nope, apply_rope(q_pe, cos, sin), k_nope, apply_rope(k_pe, cos, sin))
    qc_nope, qc_pe, kc_nope, vc, kc_pe = project(p_ctx)
    qc, kc = assemble(qc_nope, qc_pe, kc_nope, kc_pe)
    scale = (MLA_NOPE + MLA_ROPE) ** -0.5
    o = blocked_global_attention(q, k, v, kc, vc, scale)
    o_ctx = merge_heads(dense_ctx_attention(qc, kc, vc, scale)) if need_ctx else None
    return merge_heads(o), o_ctx

def swa_mixer(p_lat, p_ctx, sink, need_ctx):
    q, k, v = split_qkv(p_lat, SWA_HEADS, SWA_KV_HEADS, SWA_DIM)
    qc, kc, vc = split_qkv(p_ctx, SWA_HEADS, SWA_KV_HEADS, SWA_DIM)
    cos, sin = rope_tables(q.shape[2], SWA_DIM)
    q, k = apply_rope(q, cos, sin), apply_rope(k, cos, sin)
    sink_g = sink.reshape(SWA_KV_HEADS, SWA_HEADS // SWA_KV_HEADS)
    scale = SWA_DIM ** -0.5
    o = banded_window_attention(group_heads(q, SWA_KV_HEADS), k, v, kc, vc, sink_g, scale)
    o_ctx = (merge_heads(dense_ctx_attention(group_heads(qc, SWA_KV_HEADS), kc, vc, scale, sink_g))
             if need_ctx else None)
    return merge_heads(o), o_ctx

def na_mixer(p_lat, p_ctx, rpb, need_ctx):
    q, k, v = split_qkv(p_lat, NA_HEADS, NA_HEADS, NA_DIM)
    qc, kc, vc = split_qkv(p_ctx, NA_HEADS, NA_HEADS, NA_DIM)
    b, h, s, d = q.shape
    rows = s // GRID_W
    kh = min(NA_KH, rows)
    scale = d ** -0.5
    n_ctx = kc.shape[2]
    qg = q.reshape(b, h, rows, GRID_W, d)
    kg = k.reshape(b, h, rows, GRID_W, d)
    vg = v.reshape(b, h, rows, GRID_W, d)
    cols = jnp.arange(GRID_W)
    col_start = jnp.clip(cols - NA_KW // 2, 0, GRID_W - NA_KW)
    col_mask = (cols[None, :] >= col_start[:, None]) & (cols[None, :] < col_start[:, None] + NA_KW)
    mask = jnp.broadcast_to(col_mask[:, None, :], (GRID_W, kh, GRID_W)).reshape(GRID_W, kh * GRID_W)
    dc_idx = jnp.clip(cols[None, :] - cols[:, None], -(NA_KW - 1), NA_KW - 1) + NA_KW - 1

    def row_block(args):
        qi, r = args
        rs = jnp.clip(r - kh // 2, 0, rows - kh)
        kr = lax.dynamic_slice_in_dim(kg, rs, kh, axis=2).reshape(b, h, kh * GRID_W, d)
        vr = lax.dynamic_slice_in_dim(vg, rs, kh, axis=2).reshape(b, h, kh * GRID_W, d)
        dr_idx = rs + jnp.arange(kh) - r + NA_KH - 1
        bias = rpb[:, dr_idx[None, :, None], dc_idx[:, None, :]].reshape(h, GRID_W, kh * GRID_W)
        s_loc = jnp.einsum('bhqd,bhkd->bhqk', qi, kr).astype(jnp.float32) * scale + bias.astype(jnp.float32)
        s_loc = jnp.where(mask, s_loc, NEG_INF)
        s_ctx = jnp.einsum('bhqd,bhkd->bhqk', qi, kc).astype(jnp.float32) * scale
        p = jax.nn.softmax(jnp.concatenate([s_ctx, s_loc], axis=-1), axis=-1).astype(vr.dtype)
        return (jnp.einsum('bhqk,bhkd->bhqd', p[..., :n_ctx], vc)
                + jnp.einsum('bhqk,bhkd->bhqd', p[..., n_ctx:], vr))

    o = lax.map(row_block, (qg.transpose(2, 0, 1, 3, 4), jnp.arange(rows)))
    o = o.transpose(1, 2, 0, 3, 4).reshape(b, h, s, d)
    o_ctx = merge_heads(dense_ctx_attention(qc[:, :, None], kc, vc, scale)) if need_ctx else None
    return merge_heads(o), o_ctx

def gqa_mixer(p_lat, p_ctx, q_g, k_g, need_ctx):
    q, k, v = split_qkv(p_lat, GQA_HEADS, GQA_KV_HEADS, GQA_DIM)
    qc, kc, vc = split_qkv(p_ctx, GQA_HEADS, GQA_KV_HEADS, GQA_DIM)
    q, k = rms_norm(q, q_g), rms_norm(k, k_g)
    qc, kc = rms_norm(qc, q_g), rms_norm(kc, k_g)
    cos, sin = rope_tables(q.shape[2], GQA_DIM)
    q, k = apply_rope(q, cos, sin), apply_rope(k, cos, sin)
    scale = GQA_DIM ** -0.5
    o = blocked_global_attention(group_heads(q, GQA_KV_HEADS), k, v, kc, vc, scale)
    o_ctx = (merge_heads(dense_ctx_attention(group_heads(qc, GQA_KV_HEADS), kc, vc, scale))
             if need_ctx else None)
    return merge_heads(o), o_ctx

def conv_ffn(h, w_up, conv_w, conv_b, w_down):
    u = h @ w_up
    gate, val = u[..., :D_FF], u[..., D_FF:]
    n = h.shape[1]
    half = CONV_W // 2
    gp = jnp.pad(gate, ((0, 0), (half, half), (0, 0)))
    acc = conv_b
    for i in range(CONV_W):
        acc = acc + gp[:, i:i + n] * conv_w[i]
    return (jax.nn.gelu(acc) * val) @ w_down

def setup_inputs(seed: int = 0) -> dict:
    key = jax.random.key(seed)
    ks = jax.random.split(key, 32)
    f32 = jnp.float32
    n_even = (DEPTH + 1) // 2
    n_odd = DEPTH // 2

    def w(k, shape, fan_in):
        return jax.random.normal(k, shape, f32) * (fan_in ** -0.5)

    def gain(k, shape):
        return 1.0 + 0.05 * jax.random.normal(k, shape, f32)

    def small(k, shape, s):
        return s * jax.random.normal(k, shape, f32)

    return {
        'x': jax.random.normal(ks[0], (BATCH, SEQ, D_MODEL), f32),
        'c': jax.random.normal(ks[1], (BATCH, D_MODEL), f32),
        'ctx': jax.random.normal(ks[2], (BATCH, CTX_LEN, D_MODEL), f32),
        'c_ctx': jax.random.normal(ks[3], (D_MODEL,), f32),
        'ada_w': w(ks[4], (DEPTH, D_MODEL, 6 * D_MODEL), D_MODEL),
        'ada_b': small(ks[5], (DEPTH, 6 * D_MODEL), 0.02),
        'pre_mix_g': gain(ks[6], (DEPTH, D_MODEL)),
        'post_mix_g': gain(ks[7], (DEPTH, D_MODEL)),
        'pre_ffn_g': gain(ks[8], (DEPTH, D_MODEL)),
        'post_ffn_g': gain(ks[9], (DEPTH, D_MODEL)),
        'ffn_up': w(ks[10], (DEPTH, D_MODEL, 2 * D_FF), D_MODEL),
        'ffn_conv_w': w(ks[11], (DEPTH, CONV_W, D_FF), CONV_W),
        'ffn_conv_b': small(ks[12], (DEPTH, D_FF), 0.02),
        'ffn_down': w(ks[13], (DEPTH, D_FF, D_MODEL), D_FF),
        'even_w_in': w(ks[14], (n_even, D_MODEL, EVEN_IN), D_MODEL),
        'even_w_out': w(ks[15], (n_even, EVEN_MIX, D_MODEL), EVEN_MIX),
        'mla_q_norm_g': gain(ks[16], (n_even, MLA_Q_RANK)),
        'mla_w_uq': w(ks[17], (n_even, MLA_Q_RANK, MLA_HEADS * (MLA_NOPE + MLA_ROPE)), MLA_Q_RANK),
        'mla_kv_norm_g': gain(ks[18], (n_even, MLA_KV_RANK)),
        'mla_w_ukv': w(ks[19], (n_even, MLA_KV_RANK, MLA_HEADS * (MLA_NOPE + MLA_V)), MLA_KV_RANK),
        'swa_sink': jax.random.normal(ks[20], (n_even, SWA_HEADS), f32),
        'odd_w_in': w(ks[21], (n_odd, D_MODEL, ODD_IN), D_MODEL),
        'odd_w_out': w(ks[22], (n_odd, ODD_MIX, D_MODEL), ODD_MIX),
        'na_rpb': small(ks[23], (n_odd, NA_HEADS, 2 * NA_KH - 1, 2 * NA_KW - 1), 0.1),
        'gqa_q_g': gain(ks[24], (n_odd, GQA_DIM)),
        'gqa_k_g': gain(ks[25], (n_odd, GQA_DIM)),
    }

def reference(x, c, ctx, c_ctx, ada_w, ada_b, pre_mix_g, post_mix_g, pre_ffn_g, post_ffn_g,
              ffn_up, ffn_conv_w, ffn_conv_b, ffn_down, even_w_in, even_w_out, mla_q_norm_g,
              mla_w_uq, mla_kv_norm_g, mla_w_ukv, swa_sink, odd_w_in, odd_w_out, na_rpb,
              gqa_q_g, gqa_k_g):
    sc = jax.nn.silu(c)
    scc = jax.nn.silu(c_ctx)
    for layer in range(DEPTH):
        need_ctx = layer < DEPTH - 1
        mod_lat = [m[:, None, :] for m in jnp.split(sc @ ada_w[layer] + ada_b[layer], 6, axis=-1)]
        mod_ctx = jnp.split(scc @ ada_w[layer] + ada_b[layer], 6, axis=-1)
        h_lat = modulate(x, pre_mix_g[layer], mod_lat[0], mod_lat[1])
        h_ctx = modulate(ctx, pre_mix_g[layer], mod_ctx[0], mod_ctx[1])
        if layer % 2 == 0:
            i = layer // 2
            p_lat = h_lat @ even_w_in[i]
            p_ctx = h_ctx @ even_w_in[i]
            a_lat, a_ctx = mla_mixer(p_lat[..., :EVEN_MLA_IN], p_ctx[..., :EVEN_MLA_IN], mla_q_norm_g[i],
                                     mla_w_uq[i], mla_kv_norm_g[i], mla_w_ukv[i], need_ctx)
            b_lat, b_ctx = swa_mixer(p_lat[..., EVEN_MLA_IN:], p_ctx[..., EVEN_MLA_IN:], swa_sink[i], need_ctx)
            w_out = even_w_out[i]
        else:
            i = layer // 2
            p_lat = h_lat @ odd_w_in[i]
            p_ctx = h_ctx @ odd_w_in[i]
            a_lat, a_ctx = na_mixer(p_lat[..., :ODD_NA_IN], p_ctx[..., :ODD_NA_IN], na_rpb[i], need_ctx)
            b_lat, b_ctx = gqa_mixer(p_lat[..., ODD_NA_IN:], p_ctx[..., ODD_NA_IN:], gqa_q_g[i], gqa_k_g[i],
                                     need_ctx)
            w_out = odd_w_out[i]
        y_lat = jnp.concatenate([a_lat, b_lat], axis=-1) @ w_out
        x = x + mod_lat[2] * rms_norm(y_lat, post_mix_g[layer])
        h = modulate(x, pre_ffn_g[layer], mod_lat[3], mod_lat[4])
        f = conv_ffn(h, ffn_up[layer], ffn_conv_w[layer], ffn_conv_b[layer], ffn_down[layer])
        x = x + mod_lat[5] * rms_norm(f, post_ffn_g[layer])
        if need_ctx:
            y_ctx = jnp.concatenate([a_ctx, b_ctx], axis=-1) @ w_out
            ctx = ctx + mod_ctx[2] * rms_norm(y_ctx, post_mix_g[layer])
            hc = modulate(ctx, pre_ffn_g[layer], mod_ctx[3], mod_ctx[4])
            fc = conv_ffn(hc, ffn_up[layer], ffn_conv_w[layer], ffn_conv_b[layer], ffn_down[layer])
            ctx = ctx + mod_ctx[5] * rms_norm(fc, post_ffn_g[layer])
    return x


_drawn_inputs = setup_inputs


def setup_inputs(seed=0):
    import zlib

    import numpy as np

    out = dict(_drawn_inputs(seed))
    spreads = {}
    factors = {'ffn_conv_b': 6.078,
     'mla_q_norm_g': 8.0,
     'mla_kv_norm_g': 2.757,
     'swa_sink': 8.0,
     'na_rpb': 8.0,
     'gqa_q_g': 8.0,
     'gqa_k_g': 8.0}
    for name, (base, spread) in spreads.items():
        noise = np.random.default_rng([zlib.crc32(name.encode()), seed]).standard_normal(out[name].shape)
        drawn = base * np.exp(spread * noise) if base else spread * noise
        out[name] = __import__('jax').numpy.asarray(drawn.astype(out[name].dtype))
    for name, factor in factors.items():
        out[name] = (out[name] * factor).astype(out[name].dtype)
    return out
```

```python
import math
from contextlib import ExitStack

import concourse.bass as bass
import numpy as np
from concourse import mybir

P = 128
D = 1024
LAT, CTX = 512, 256
ROWS = LAT + CTX
LT, NT = LAT // P, ROWS // P
KC = D // P
GRID_W = 64
EPS = 1e-6
NEG = -1e30
Q_RANK, KV_RANK, ROPE_D, NOPE = 256, 128, 32, 64
MLA_IN = Q_RANK + KV_RANK + ROPE_D
MLA_D = NOPE + ROPE_D
EVEN_IN, ODD_IN = 1184, 2560
FF = 2816
FT = FF // P
ADA_COLS = 256
ADA_UNITS = 6 * D // ADA_COLS
ADA_FIRST = 2 * D // ADA_COLS
TZ_W = 2 * GRID_W - 1
NA_ROWS = 14


class Chain:

    def __init__(self, eng, sem):
        self.eng, self.sem, self.n, self.term = eng, sem, 0, 0

    def inc(self, instruction):
        instruction.then_inc(self.sem, 1)
        self.n += 1

    def wait(self):
        self.eng.wait_ge(self.sem, self.term + self.n)


def run_loop(eng, first, last, body, chain=None, growth=0):
    if last <= first:
        return
    if last == first + 1:
        body(first)
        return
    with eng.Fori(first, last) as i:
        if chain is not None:
            start = chain.n
            chain.term = (i - first) * growth if growth else 0
        body(i)
        if chain is not None:
            assert chain.n - start == growth, (chain.n - start, growth)
            chain.term, chain.n = 0, start + growth * (last - first)


class Attention:

    def __init__(self, name, heads, d, dv, units, mix_chunk, banded=False, bias=None, sink=False):
        self.name, self.heads, self.d, self.dv, self.mix_chunk = name, heads, d, dv, mix_chunk
        self.bias, self.sink = bias, sink
        self.scale = d ** -0.5
        self.nu = units
        self.pairs = heads // 2
        self.full = units == NT
        self.units = []
        for t in range(units):
            if t >= LT:
                lo, n = 0, 0
            elif banded:
                lo = max(t - 1, 0)
                n = min(t + 2, LT) - lo
            else:
                lo, n = 0, LT
            chunks = [(c * P, lo + c) for c in range(n)] + [(LAT + c * P, LT + c) for c in range(NT - LT)]
            if n == 0:
                rounds = [chunks]
            elif banded:
                rounds = [chunks[:n], chunks[n:]]
            else:
                rounds = [chunks[:3], chunks[3:]]
            self.units.append((t, lo, n, rounds))
        self.unit_rounds = [len(u[3]) for u in self.units]
        self.q_rounds = [[0, 1, 2], [3, 4, 5]] if self.full else [[0, 1], [2, 3]]
        self.k_rounds = [[0, 1, 2], [3, 4, 5]]
        self.head_rounds = sum(self.unit_rounds) + 4
        self.total_rounds = 4 + (heads - 1) * self.head_rounds + sum(self.unit_rounds)
        self.load_inc = 16 * {"mla": 4, "swa": 3, "na": 5, "gqa": 3}[name]
        self.acols = ROWS if self.full else LAT
        assert self.head_rounds % 2 == 0 and self.total_rounds % 2 == 0 and units % 2 == 0

    def _before(self, j, last_head):
        return sum(self.unit_rounds[:j]) + (0 if last_head else 2 * min(j, 2))

    def unit_round(self, h, j, last_head):
        return h * self.head_rounds + (4 + self._before(j, last_head))

    def prep_round(self, h, n):
        if isinstance(h, int) and h == 0:
            return n
        j = n // 2
        return (h - 1) * self.head_rounds + (4 + self._before(j, False) + self.unit_rounds[j] + n % 2)

    def prep_end(self, h):
        return self.prep_round(h, 3) + 1


def build(nc, I, C, out):
    fp32, f32r = mybir.dt.float32, mybir.dt.float32r
    ALU, ACT, AX = mybir.AluOpType, mybir.ActivationFunctionType, mybir.AxisListType
    ds = bass.ds

    def scratch(name, shape):
        return nc.dram_tensor(name, shape, fp32)

    proj = [scratch("proj_even", [ROWS, EVEN_IN]), scratch("proj_odd", [ROWS, ODD_IN])]
    mla_q = scratch("mla_q", [ROWS, 8 * MLA_D])
    mla_kv = scratch("mla_kv", [ROWS, 8 * 2 * NOPE])
    xs = [scratch(f"x_after_{n}", [ROWS, D]) for n in ("mix0", "ffn0", "mix1")]
    mods = scratch("mods", [2, 2, 6 * D])
    toeplitz = scratch("toeplitz", [8 * 15, GRID_W * TZ_W])

    ctx = ExitStack()
    with ctx:
        def sb(name, shape, dt=fp32):
            return ctx.enter_context(nc.sbuf_tensor(name, shape, dt))

        def sem(name):
            return ctx.enter_context(nc.semaphore(name))

        G_EL, Y_EL = FT * ROWS, NT * D
        arena_at = (nc.sbuf_base + 31) // 32 * 32
        arena = sb("arena", [P, G_EL + Y_EL])
        act_hi, act_lo = sb("act_hi", [P, KC, ROWS], f32r), sb("act_lo", [P, KC, ROWS], f32r)
        w_raw = sb("w_raw", [P, 2, 2048])
        w_hi, w_lo = sb("w_hi", [P, 2, 2048], f32r), sb("w_lo", [P, 2, 2048], f32r)
        ident = sb("ident", [P, P])
        rope = {w: sb(f"rope{w}", [P, LT, 2, w]) for w in (16, 32, 64)}
        band = sb("band", [P, 3 * P])
        colmask = sb("colmask", [P, GRID_W])
        conv = sb("conv", [P, 2, FT, 4])
        cvec, cexp = sb("cvec", [P, KC, 2]), sb("cexp", [P, KC, 2])
        silu = sb("silu", [P, KC, 2])
        g_mla = sb("g_mla", [P, Q_RANK + KV_RANK])
        g_gqa = sb("g_gqa", [P, 2, P])
        sinks, sinks8 = sb("sinks", [P, 8]), sb("sinks8", [P, 8])
        ada_bias, ada_row = sb("ada_bias", [2, 2, ADA_COLS]), sb("ada_row", [2, 2, ADA_COLS])
        rpb = sb("rpb", [8 * 15, P])
        flag = sb("flag", [P, 1])
        mhalf = sb("mhalf", [P, 8])
        ssy, ssx = sb("ssy", [P, NT]), sb("ssx", [P, NT])
        rsy, rsx = sb("rsy", [P, NT]), sb("rsx", [P, NT])
        ssh, rsh = sb("ssh", [P, 2, 4]), sb("rsh", [P, 2, 4])
        mx, nb = sb("mx", [P, 2, 2]), sb("nb", [P, 2])
        ex, es = sb("ex", [P, 2, 2]), sb("es", [P, 2])
        rsum, rinv = sb("rsum", [P, 2]), sb("rinv", [P, 2])

        G = arena[:, 0:G_EL].rearrange("p (t r) -> p t r", t=FT)
        Y = arena[:, G_EL:G_EL + Y_EL].rearrange("p (t d) -> p t d", t=NT)
        conv_acc = arena[:, G_EL:G_EL + 2 * ROWS].rearrange("p (s r) -> p s r", s=2)
        ada_raw = arena[:, G_EL + 2 * ROWS:G_EL + 2 * ROWS + 4096].rearrange("p (s k c) -> p s k c", s=2, k=KC)

        def kilo(n):
            return arena[:, n * D:(n + 1) * D]
        mod_row = [[kilo(2 * m + v) for v in range(2)] for m in range(3)]
        x_in = [kilo(6), kilo(7)]
        x_new = [kilo(8), kilo(9)]
        h_tok = [kilo(10), kilo(11)]

        at = [arena_at]

        def split(name, shape):
            n = math.prod(shape[1:])
            t = nc.alloc_sbuf_tensor_at(name, shape, f32r, offset=at[0])
            at[0] += 4 * n
            return t
        c_at = at[0]
        qt = [[split(f"qt_{x}{i}", [P, ROWS]) for x in ("hi", "lo")] for i in range(2)]
        kt = [[split(f"kt_{x}{i}", [P, ROWS]) for x in ("hi", "lo")] for i in range(2)]
        vs = [[split(f"v_{x}{i}", [P, NT, P]) for x in ("hi", "lo")] for i in range(2)]
        pt = [[split(f"pt_{x}{i}", [P, NT, P]) for x in ("hi", "lo")] for i in range(2)]
        at_end = at[0]
        at[0] = c_at
        lat_t = [split(f"latent_{x}", [P, 3, ROWS]) for x in ("hi", "lo")]
        at[0] = at_end
        cur = [(at_end - arena_at) // 4]

        def plain(n):
            v = arena[:, cur[0]:cur[0] + n]
            cur[0] += n
            assert cur[0] <= G_EL + Y_EL
            return v
        plain_at = cur[0]
        q_raw = [plain(NT * P) for _ in range(2)]
        k_raw = [plain(NT * P) for _ in range(2)]
        v_raw = [plain(NT * P) for _ in range(2)]
        prob = [plain(ROWS) for _ in range(2)]
        biased = [plain(LAT) for _ in range(2)]
        na_bias = [plain(NA_ROWS * GRID_W) for _ in range(2)]
        cur[0] = plain_at - 2 * D
        stage = [plain(512) for _ in range(4)]
        mla_in = [plain(MLA_IN) for _ in range(NT)]
        tmp = [plain(512) for _ in range(2)]
        assert cur[0] <= G_EL + 2 * ROWS

        ps = ctx.enter_context(nc.psum_tensor("ps", [P, 8 * 512], fp32))

        def bank(b, n=512, off=0):
            return ps[:, b * 512 + off:b * 512 + off + n]

        const_in = sem("const_in")
        passed = sem("passed")
        sc_ready = sem("sc_ready")
        w_in = [sem("w_in0"), sem("w_in1")]
        w_hi_done, w_lo_done = sem("w_hi_done"), sem("w_lo_done")
        ada_in = [sem("ada_in0"), sem("ada_in1")]
        ada_out = [sem("ada_out0"), sem("ada_out1")]
        mm_done = sem("mm_done")
        acc_evac = sem("acc_evac")
        t_done, t_hi, t_free = sem("t_done"), sem("t_hi"), sem("t_free")
        mod_in, mod_ready = sem("mod_in"), sem("mod_ready")
        gain_in, gain_used = sem("gain_in"), sem("gain_used")
        x_ld = [sem("x_ld0"), sem("x_ld1")]
        x_st = [sem("x_st0"), sem("x_st1")]
        sum_y, rs_y, y_scaled, x_added = sem("sum_y"), sem("rs_y"), sem("y_scaled"), sem("x_added")
        sum_x, rs_x, h_scaled, h_ready = sem("sum_x"), sem("rs_x"), sem("h_scaled"), sem("h_ready")
        squares, head_rs = sem("squares"), sem("head_rs")
        staged = sem("staged")
        stage_out = [sem(f"stage_out{i}") for i in range(4)]
        kpe_out = sem("kpe_out")
        head_in = [sem("head_in0"), sem("head_in1")]
        v_split, bias_ready = sem("v_split"), sem("bias_ready")
        s_done, mx_done, exp_done, rc_done, p_scaled = (sem("s_done"), sem("mx_done"), sem("exp_done"),
                                                        sem("rc_done"), sem("p_scaled"))
        pv_done, o_hi, o_lo = sem("pv_done"), sem("o_hi"), sem("o_lo")
        centre, taps, gelu, gated = sem("centre"), sem("taps"), sem("gelu"), sem("gated")
        g_hi, g_lo = sem("g_hi"), sem("g_lo")
        dve_self, act_self, pool_self = sem("dve_self"), sem("act_self"), sem("pool_self")
        tz_in, tz_out = sem("tz_in"), sem("tz_out")

        block = ctx.enter_context(nc.Block())

        MLA = Attention("mla", 8, MLA_D, 64, NT, 0)
        SWA = Attention("swa", 8, 64, 64, NT, 4, banded=True, bias="band", sink=True)
        NA = Attention("na", 8, 64, 64, LT, 0, bias="na")
        GQA = Attention("gqa", 4, 128, 128, LT, 4)
        ATT = [[MLA, SWA], [NA, GQA]]

        head_fills = {"mla": [0, 0]}
        for prev, a in ((MLA, SWA), (SWA, NA), (NA, GQA)):
            head_fills[a.name] = [n + prev.heads // 2 * prev.load_inc for n in head_fills[prev.name]]

        IN_CHUNKS = [[(0, MLA_IN, range(NT)), (MLA_IN, 512, range(NT)), (MLA_IN + 512, 256, range(NT))],
                     [(0, 512, range(LT)), (512, 512, range(NT)), (1024, 512, range(NT)),
                      (1536, 512, range(LT)), (2048, 512, range(NT))]]
        ROWT = [NT, LT]

        def column(v):
            return v.rearrange("(k p) -> p k", p=P)
        CONSTS = [(cvec[:, :, 0], column(I["c"][0, :])), (cvec[:, :, 1], column(I["c_ctx"])),
                  (ident[:, :], C["ident"]), (band[:, :], C["band"]), (colmask[:, :], C["colmask"])]
        CONSTS += [(rope[w][:, :, :, :], C[f"rope{w}"]) for w in rope]
        CONSTS += [(conv[:, l, :, i], column(I["ffn_conv_w"][l, i, :])) for l in range(2) for i in range(3)]
        CONSTS += [(conv[:, l, :, 3], column(I["ffn_conv_b"][l, :])) for l in range(2)]
        CONSTS += [(g_mla[:, 0:Q_RANK], I["mla_q_norm_g"].to_broadcast([P, Q_RANK])),
                   (g_mla[:, Q_RANK:], I["mla_kv_norm_g"].to_broadcast([P, KV_RANK])),
                   (g_gqa[:, 0, :], I["gqa_q_g"].to_broadcast([P, P])),
                   (g_gqa[:, 1, :], I["gqa_k_g"].to_broadcast([P, P])),
                   (sinks[:, :], I["swa_sink"].to_broadcast([P, 8]))]
        CONST_IN = 16 * len(CONSTS)

        def att_growth(a):
            return dict(t=a.total_rounds, th=a.total_rounds, s=a.heads * a.nu, hd=a.heads)

        def norm_growth(tiles, y, h, streams):
            return dict(t=2 * tiles * h, th=2 * tiles * h, y=tiles * y, h=tiles * h, xl=tiles, xs=tiles * y,
                        mod=streams * (y + 2 * h), gain=y + h, nm=1)

        N0, N1 = ROWT
        accs = [sum(len(c[2]) for c in IN_CHUNKS[l]) for l in range(2)]
        PHASES = [
            ("ada", dict(t=ADA_FIRST)),
            ("norm0", norm_growth(NT, 0, 1, 2)),
            ("in0", dict(t=22, th=NT, mm=2 * accs[0] + 4 * NT, w=8, ev=accs[0] + 4 * NT,
                         st=accs[0] - NT + 4 * NT, nsq=NT)),
            ("mla", att_growth(MLA)), ("swa", att_growth(SWA)),
            ("out0", dict(mm=4 * N0, w=4, ev=2 * N0)),
            ("norm1", norm_growth(N0, 1, 1, 2)),
            ("up0", dict(t=ADA_UNITS, mm=2 * FT, w=FT, f=FT)),
            ("down0", dict(mm=FT * N0, w=FT, ev=2 * N0, g=FT)),
            ("norm2", norm_growth(NT, 1, 1, 2)),
            ("in1", dict(mm=2 * accs[1], w=10, ev=accs[1], st=accs[1], nsq=LT + NT)),
            ("na", att_growth(NA)), ("gqa", att_growth(GQA)),
            ("out1", dict(mm=4 * N1, w=4, ev=2 * N1)),
            ("norm3", norm_growth(N1, 1, 1, 1)),
            ("up1", dict(mm=2 * FT, w=FT, f=FT)),
            ("down1", dict(mm=2 * FT // 2 * N1, w=FT, ev=2 * N1, g=FT)),
            ("norm4", norm_growth(N1, 1, 0, 1)),
        ]
        BASE, total = {}, dict.fromkeys("t th mm w ev st s hd y h xl xs mod gain nm nsq f g".split(), 0)
        for name, growth in PHASES:
            BASE[name] = dict(total)
            for k, v in growth.items():
                total[k] += v

        base_staged = [0, accs[0] + 4 * NT]

        def base(name, what):
            return BASE[name][what]

        PV0 = OL0 = 1

        ADA_IN0 = list(range(8)) + list(range(14, 22))

        def ada_round(layer, g):
            if layer == 0:
                return g if g < ADA_FIRST else base("in0", "t") + ADA_IN0[g - ADA_FIRST]
            return base("up0", "t") + g

        def at_least(eng, sem, value):
            if not (isinstance(value, int) and value <= 0):
                eng.wait_ge(sem, value)

        def wait_apart(eng, *waits):
            for s, v in waits:
                eng.wait_ge(s, v)
                eng.sem_inc(passed, 1)

        NORMS = {
            "norm0": (None, (0, 1), (0, 0), None, ("pre_mix_g", 0), None, None),
            "norm1": ((0, 2), (0, 4), (0, 3), ("post_mix_g", 0), ("pre_ffn_g", 0), None, 0),
            "norm2": ((0, 5), (1, 1), (1, 0), ("post_ffn_g", 0), ("pre_mix_g", 1), 0, 1),
            "norm3": ((1, 2), (1, 4), (1, 3), ("post_mix_g", 1), ("pre_ffn_g", 1), 1, 2),
            "norm4": ((1, 5), None, None, ("post_ffn_g", 1), None, 2, "out"),
        }
        NORM_TILES = {"norm0": NT, "norm1": N0, "norm2": NT, "norm3": N1, "norm4": N1}
        NORM_STREAMS = {"norm0": 2, "norm1": 2, "norm2": 2, "norm3": 1, "norm4": 1}
        DOWN_TAIL = 20

        def x_source(name, t):
            k = NORMS[name][5]
            if k is None:
                return I["x"][0, t * P:(t + 1) * P, :] if t < LT else I["ctx"][0, (t - LT) * P:(t - LT + 1) * P, :]
            return xs[k][t * P:(t + 1) * P, :]

        def up_cols(t, half):
            return t * P + half * FF

        @block.sync
        def _(sp):
            def raw_free(u):
                at_least(sp, w_lo_done, u - 1)

            def k_unit(u, w, k0, kn, c0, cn):
                raw_free(u)
                v = w.rearrange("(k p) c -> p k c", p=P)
                dst = w_raw[:, u % 2, 0:kn * cn].rearrange("p (k c) -> p k c", c=cn)
                if kn == 1:
                    for a, b in ((0, cn // 2), (cn // 2, cn)):
                        sp.dma_start(dst[:, 0, a:b], v[:, k0, c0 + a:c0 + b]).then_inc(w_in[u % 2], 16)
                else:
                    for a, b in ((0, kn // 2), (kn // 2, kn)):
                        sp.dma_start(dst[:, a:b, :], v[:, k0 + a:k0 + b, c0:c0 + cn]).then_inc(w_in[u % 2], 16)

            def up_unit(layer, t, slot):
                v = I["ffn_up"][layer].rearrange("(k p) c -> p k c", p=P)
                for half in range(2):
                    dst = w_raw[:, slot, half * 1024:(half + 1) * 1024].rearrange("p (k c) -> p k c", k=KC)
                    sp.dma_start(dst, v[:, :, ds(up_cols(t, half), P)]).then_inc(w_in[slot], 16)

            def down_unit(layer, k, half, slot):
                for j in range(2):
                    src = I["ffn_down"][layer][ds((k + j) * P, P), half * 512:(half + 1) * 512]
                    sp.dma_start(w_raw[:, slot, j * 512:(j + 1) * 512], src).then_inc(w_in[slot], 16)

            def ada_unit(layer, g, slot):
                v = I["ada_w"][layer].rearrange("(k p) c -> p k c", p=P)
                sp.dma_start(ada_raw[:, slot], v[:, :, ds(g * ADA_COLS, ADA_COLS)]).then_inc(ada_in[slot], 16)
                b = I["ada_b"][layer:layer + 1, ds(g * ADA_COLS, ADA_COLS)]
                sp.dma_start(ada_bias[:, slot], b.to_broadcast([2, ADA_COLS])).then_inc(ada_in[slot], 16)

            def norm_loads(name):
                gate, scale, shift, post, pre, _, _ = NORMS[name]
                last = {"norm0": 8, "norm1": 24, "norm2": 32, "norm3": 48, "norm4": 48}[name]
                for s in range(2):
                    sp.wait_ge(ada_out[s], 16 * last // 2)
                for m, lc in enumerate((gate, scale, shift)):
                    if lc is None:
                        continue
                    for v in range(NORM_STREAMS[name]):
                        src = mods[lc[0], v:v + 1, lc[1] * D:(lc[1] + 1) * D]
                        sp.dma_start(mod_row[m][v], src.to_broadcast([P, D])).then_inc(mod_in, 16)
                for n, g in enumerate((post, pre)):
                    if g is not None:
                        src = I[g[0]][g[1]:g[1] + 1, :]
                        sp.dma_start(h_tok[n], src.to_broadcast([P, D])).then_inc(gain_in, 16)

            def x_loads(name, tiles):
                for t in tiles:
                    if t >= 2:
                        if NORMS[name][0] is None:
                            sp.wait_ge(h_scaled, base(name, "h") + t - 1)
                        else:
                            sp.wait_ge(x_added, base(name, "y") + t - 1)
                    if t < 2 and NORMS[name][5] is not None:
                        for s in range(2):
                            sp.wait_ge(x_st[s], 16 * base(name, "xs") // 2)
                    sp.dma_start(x_in[t % 2], x_source(name, t)).then_inc(x_ld[t % 2], 16)

            def head_loads(name, a, before):
                def rows(src, c, n, tiles=NT):
                    return src[0:tiles * P, ds(c, n)].rearrange("(t p) c -> p t c", p=P)

                def load(h, s):

                    def put(dst, src):
                        sp.dma_start(dst, src).then_inc(head_in[s], 16)
                    q = q_raw[s][:, 0:NT * a.d].rearrange("p (t c) -> p t c", c=a.d)[:, 0:a.nu]
                    k = k_raw[s][:, 0:NT * a.d].rearrange("p (t c) -> p t c", c=a.d)
                    v = v_raw[s][:, 0:NT * a.dv].rearrange("p (t c) -> p t c", c=a.dv)
                    if a.name == "mla":
                        put(q, rows(mla_q, h * MLA_D, MLA_D))
                        put(k[:, :, 0:NOPE], rows(mla_kv, h * 2 * NOPE, NOPE))
                        put(k[:, :, NOPE:MLA_D], rows(proj[0], Q_RANK + KV_RANK, ROPE_D))
                        put(v, rows(mla_kv, h * 2 * NOPE + NOPE, NOPE))
                    elif a.name == "swa":
                        kv = (h // 4) * 64 if isinstance(h, int) else h * 0
                        put(q, rows(proj[0], h * 64 + MLA_IN, 64))
                        put(k, rows(proj[0], kv + MLA_IN + 512, 64))
                        put(v, rows(proj[0], kv + MLA_IN + 640, 64))
                    elif a.name == "na":
                        put(q, rows(proj[1], h * 64, 64, LT))
                        put(k, rows(proj[1], h * 64 + 512, 64))
                        put(v, rows(proj[1], h * 64 + 1024, 64))
                        for rl in range(2):
                            src = toeplitz[ds(h * 15 + (1 - rl), NA_ROWS),
                                           GRID_W - 1:GRID_W - 1 + GRID_W * (TZ_W - 1)]\
                                .rearrange("r (c x) -> c r x", x=TZ_W - 1)[:, :, 0:GRID_W]
                            dst = na_bias[s][rl * GRID_W:(rl + 1) * GRID_W, :].rearrange("p (r c) -> p r c", c=GRID_W)
                            put(dst, src)
                    else:
                        put(q, rows(proj[1], h * P + 1536, P, LT))
                        kv = (h // 2) * P
                        put(k, rows(proj[1], kv + 2048, P))
                        put(v, rows(proj[1], kv + 2048 + 256, P))

                for h in range(2):
                    if before is not None:
                        pn, pa = before
                        hp = pa.heads - 2 + h
                        sp.wait_ge(t_free, base(pn, "t") + pa.prep_end(hp))
                        sp.wait_ge(v_split, base(pn, "hd") + hp + 1)
                    load(h, h)

                def pair(i):
                    for s in range(2):
                        h = i * 2 + s
                        waits = [(t_free, a.prep_end(h - 2) + base(name, "t")),
                                 (v_split, h + (base(name, "hd") - 1))]
                        if a.bias == "na":
                            waits.append((mx_done, (h - 1) * a.nu + base(name, "s")))
                        wait_apart(sp, *waits)
                        load(h, s)
                if a.name in ("swa", "gqa"):
                    for i in range(1, a.pairs):
                        pair(i)
                else:
                    pair(1)
                    run_loop(sp, 2, a.pairs, pair)

            for g in range(ADA_FIRST):
                if g >= 2:
                    sp.wait_ge(t_free, ada_round(0, g - 2) + 1)
                ada_unit(0, g, g % 2)
            for n in range(2):
                k_unit(n, I["even_w_in"][0], 4 * n, 4, 0, MLA_IN)
            norm_loads("norm0")
            x_loads("norm0", range(NT))
            units = [(I["even_w_in"][0], 4 * n, 4, c, cn) for c, cn, _ in IN_CHUNKS[0] for n in range(2)]
            units += [(I["mla_w_uq"][0], 0, 2, 0, 8 * MLA_D), (I["mla_w_ukv"][0], 0, 1, 0, 16 * NOPE)]
            units += [(I["even_w_out"][0], 4 * n, 4, c, 512) for c in (0, 512) for n in range(2)]
            for n in range(8):
                for g in range(ADA_FIRST + 2 * n, ADA_FIRST + 2 * n + 2):
                    sp.wait_ge(t_free, ada_round(0, g - 2) + 1)
                    ada_unit(0, g, g % 2)
                k_unit(n + 2, *units[n + 2])
            for u in (10, 11):
                k_unit(u, *units[u])
            for layer in range(2):
                names = [("mla", "swa"), ("na", "gqa")][layer]
                nm, nf = ("norm1", "norm2") if layer == 0 else ("norm3", "norm4")
                for s in range(4):
                    n_st = base(names[0], "st")
                    sp.wait_ge(stage_out[s], 16 * ((n_st + 3 - s) // 4))
                if layer == 0:
                    sp.wait_ge(kpe_out, 16 * NT)
                else:
                    sp.wait_ge(tz_out, 16)
                head_loads(names[0], ATT[layer][0], None)
                head_loads(names[1], ATT[layer][1], (names[0], ATT[layer][0]))
                sp.wait_ge(o_lo, OL0 + base(nm, "hd"))
                norm_loads(nm)
                x_loads(nm, range(2))
                up, w_up, w_down = f"up{layer}", base(f"up{layer}", "w"), base(f"down{layer}", "w")
                for t in range(2):
                    raw_free(w_up + t)
                    up_unit(layer, t, t)
                x_loads(nm, range(2, ROWT[layer]))
                if layer == 0:
                    sp.wait_ge(x_added, base(nm, "y") + NT)
                    for g in range(2):
                        ada_unit(1, g, g)

                def up_trip(i, weights=True):
                    for k in range(2):
                        if layer == 0:
                            wait_apart(sp, (t_free, i * 2 + (base(up, "t") + k + 1)))
                            ada_unit(1, i * 2 + (k + 2), k)
                        if weights:
                            wait_apart(sp, (w_lo_done, i * 2 + (w_up + 2 + k - 1)))
                            up_unit(layer, i * 2 + (k + 2), k)
                run_loop(sp, 0, FT // 2 - 1, up_trip)
                up_trip(FT // 2 - 1, False)
                for half in range(2):
                    w0 = w_down + half * (FT // 2)

                    def down_trip(i):
                        for k in range(2):
                            wait_apart(sp, (w_lo_done, i * 2 + (w0 + k - 1)))
                            down_unit(layer, i * 4 + 2 * k, half, (w0 + k) % 2)
                    run_loop(sp, 0, FT // 4, down_trip)
                    sp.wait_ge(w_lo_done, w0 + FT // 2 - 1 - 1)
                    down_unit(layer, 4 * (FT // 4), half, (w0 + FT // 2 - 1) % 2)
                if layer == 0:
                    w_in1 = base("in1", "w")
                    units = [(I["odd_w_in"][0], 4 * n, 4, c, cn) for c, cn, _ in IN_CHUNKS[1] for n in range(2)]
                    units += [(I["odd_w_out"][0], 4 * n, 4, c, 512) for c in (0, 512) for n in range(2)]
                    for n in range(2):
                        k_unit(w_in1 + n, *units[n])
                sp.wait_ge(mm_done, base(f"down{layer}", "mm") + DOWN_TAIL * ROWT[layer])
                norm_loads(nf)
                x_loads(nf, range(NORM_TILES[nf]))
                if layer == 0:
                    for n in range(2, len(units)):
                        k_unit(w_in1 + n, *units[n])

        @block.tensor
        def _(pe):
            mm = nc.tensor.matmul

            def three(out_, s_hi, s_lo, m_hi, m_lo, start=True, stop=True):
                mm(out_, s_hi, m_hi, start=start, stop=False)
                mm(out_, s_hi, m_lo, start=False, stop=False)
                return mm(out_, s_lo, m_hi, start=False, stop=stop)

            def ring_free(r):
                at_least(pe, t_free, r - 1)

            def ada_mm(use, r, slot, inc=None):
                ring_free(r)
                pe.wait_ge(ada_in[slot], use * 32)
                o = bank(6 + slot, ADA_COLS)[0:2, :]
                for k in range(KC):
                    last = mm(o, silu[:, k, :], ada_raw[:, slot, k, :], start=k == 0, stop=k == KC - 1)
                last.then_inc(t_done, 1)

            def turn(r, rb, srcs, pn=P):
                if pn < P and not (isinstance(r, int) and r <= 1):
                    wait_apart(pe, (t_free, r - 1))
                else:
                    ring_free(r)
                for n, src in enumerate(srcs):
                    last = nc.tensor.transpose(bank(6 + rb % 2)[0:pn, n * P:(n + 1) * P], src, ident[:, :])
                last.then_inc(t_done, 1)

            def weights(u):
                pe.wait_ge(w_lo_done, u + 1)

            def norm_turns(name):
                for t in range(NORM_TILES[name]):
                    pe.wait_ge(h_ready, base(name, "h") + t + 1)
                    for half in range(2):
                        r = base(name, "t") + 2 * t + half
                        turn(r, r, [h_tok[t % 2][:, (4 * half + k) * P:(4 * half + k + 1) * P] for k in range(4)])

            last_use = [0] * 6

            def bank_free(b):
                at_least(pe, acc_evac, last_use[b])

            def unit_mm(slot, tiles, kn, n, lhs, k0, start, stop, wk0=0, after=None):
                wh = w_hi[:, slot, :]
                wl = w_lo[:, slot, :]
                for b, t in enumerate(tiles):
                    if start:
                        bank_free(b)
                    for k in range(kn):
                        rows = slice(t * P, (t + 1) * P)
                        cols = slice((wk0 + k) * n, (wk0 + k + 1) * n)
                        last = three(bank(b, n), lhs[0][:, k0 + k, rows], lhs[1][:, k0 + k, rows],
                                     wh[:, cols], wl[:, cols], start and k == 0, stop and k == kn - 1)
                    last.then_inc(mm_done, 1)
                    if after is not None:
                        after(b)

            def in_projection(layer):
                name = f"in{layer}"
                u, ev = base(name, "w"), base(name, "ev")
                pe.wait_ge(t_free, base(name, "t"))
                t0 = base(name, "t")
                for ci, (c0, cn, tiles) in enumerate(IN_CHUNKS[layer]):
                    for n in range(2):
                        weights(u)
                        after = None
                        if layer == 0 and ci == 2 and n == 0:
                            def after(b):
                                pe.wait_ge(staged, b + 1)
                                turn(t0 + 8 + b, t0 + 8 + b,
                                     [mla_in[b][:, k * P:(k + 1) * P] for k in range(3)])
                        unit_mm(u % 2, tiles, 4, cn, (act_hi, act_lo), 4 * n, n == 0, n == 1, after=after)
                        if layer == 0:
                            for k in range(2):
                                g = ADA_FIRST + 2 * u + k
                                ada_mm(g // 2 + 1, ada_round(0, g), k)
                        u += 1
                    for b in range(len(tiles)):
                        last_use[b] = ev + b + 1
                    ev += len(tiles)
                if layer == 0:
                    pe.wait_ge(t_free, t0 + 14)
                    for kn, k0, n in ((2, 0, 384), (1, 2, 512)):
                        weights(u)
                        for half in range(2):
                            wh = w_hi[:, u % 2, 0:kn * 2 * n].rearrange("p (k c) -> p k c", k=kn)
                            wl = w_lo[:, u % 2, 0:kn * 2 * n].rearrange("p (k c) -> p k c", k=kn)
                            for b in range(NT):
                                bank_free(b)
                                last_use[b] = ev + b + 1
                                for k in range(kn):
                                    rows = slice(b * P, (b + 1) * P)
                                    cols = slice(half * n, (half + 1) * n)
                                    last = three(bank(b, n), lat_t[0][:, k0 + k, rows], lat_t[1][:, k0 + k, rows],
                                                 wh[:, k, cols], wl[:, k, cols], k == 0, k == kn - 1)
                                last.then_inc(mm_done, 1)
                            ev += NT
                        for k in range(2):
                            g = ADA_FIRST + 2 * u + k
                            ada_mm(g // 2 + 1, ada_round(0, g), k)
                        u += 1

            def attention(name, a):
                T0, S0, H0 = base(name, "t"), base(name, "s"), base(name, "hd")
                d, dv = a.d, a.dv

                def prep(h, s, rounds):
                    for n in rounds:
                        raw = (q_raw, k_raw)[n // 2][s][:, 0:NT * d].rearrange("p (t c) -> p t c", c=d)
                        tiles = (a.q_rounds, a.k_rounds)[n // 2][n % 2]
                        r = a.prep_round(h, n) + T0
                        turn(r, a.prep_round(0 if isinstance(h, int) and h == 0 else 2 + s, n) + T0,
                             [raw[:, t, :] for t in tiles], d)

                def scores(h, s, j):
                    t, lo, n, _ = a.units[j]
                    rows = slice(t * P, (t + 1) * P)
                    sb0 = (j % 2) * 2
                    regions = []
                    if n:
                        regions.append((bank(sb0, n * P), slice(lo * P, (lo + n) * P)))
                    regions.append((bank(sb0 + 1, CTX), slice(LAT, ROWS)))
                    q, k = qt[s], kt[s]
                    for qi, ki, start, stop in ((0, 0, True, False), (0, 1, False, False), (1, 0, False, True)):
                        for o, keys in regions:
                            last = mm(o, q[qi][0:d, rows], k[ki][0:d, keys], start=start, stop=stop)
                    last.then_inc(s_done, 1)

                def probs_t(h, j, last_head):
                    r = a.unit_round(h, j, last_head) + T0
                    for n, chunks in enumerate(a.units[j][3]):
                        turn(r + n, a.unit_round(0, j, last_head) + T0 + n,
                             [prob[j % 2][:, c:c + P] for c, _ in chunks])

                def pv(h, s, j):
                    chunks = [c for rnd in a.units[j][3] for c in rnd]
                    t = a.units[j][0]
                    b = 4 if a.full else 4 + s
                    o = ps[0:dv, b * 512 + t * P:b * 512 + (t + 1) * P]
                    for n, (_, key) in enumerate(chunks):
                        last = three(o, vs[s][0][:, key, 0:dv], vs[s][1][:, key, 0:dv],
                                     pt[j % 2][0][:, n, :], pt[j % 2][1][:, n, :], n == 0, n == len(chunks) - 1)
                    last.then_inc(pv_done, 1)

                def step(i, s, j, last_pair, first=False):
                    h = i * 2 + s
                    last_head = last_pair and s == 1
                    unit = h * a.nu + (S0 + j)
                    j2, s2, h2 = j + 2, s, h
                    if j2 >= a.nu:
                        j2, s2, h2 = j2 - a.nu, 1 - s, h + 1
                    if not (last_head and s2 != s):
                        if j2 == 0:
                            pe.wait_ge(t_free, a.prep_end(h2) + T0)
                        pe.wait_ge(exp_done, unit + 1)
                        scores(h2, s2, j2)
                    pe.wait_ge(p_scaled, unit + 1)
                    probs_t(h, j, last_head)
                    if not first:
                        pj, p_s, ph = (j - 1, s, h) if j else (a.nu - 1, 1 - s, h - 1)
                        pv_of(ph, p_s, pj, last_head and j > 0)
                    if j < 2 and not last_head:
                        if j == 0:
                            wait_head(i, s)
                        prep(h + 1, 1 - s, (2 * j, 2 * j + 1))

                def wait_head(i, s):
                    fills = head_fills[name]
                    if s == 0:
                        pe.wait_ge(head_in[1], i * a.load_inc + (fills[1] + a.load_inc))
                    else:
                        pe.wait_ge(head_in[0], i * a.load_inc + (fills[0] + 2 * a.load_inc))

                def pv_of(h, s, j, last_head):
                    pe.wait_ge(t_free, a.unit_round(h, j, last_head) + (T0 + a.unit_rounds[j]))
                    if j == 0:
                        pe.wait_ge(v_split, h + (H0 + 1))
                        pe.wait_ge(o_lo, h + (H0 + OL0 - (0 if a.full else 1)))
                    pv(h, s, j)

                at_least(pe, acc_evac, base(name, "ev"))
                at_least(pe, o_lo, OL0 + H0)
                pe.wait_ge(head_in[0], head_fills[name][0] + a.load_inc)
                prep(0, 0, range(4))
                pe.wait_ge(t_free, T0 + 4)
                for j in range(2):
                    at_least(pe, exp_done, S0)
                    scores(0, 0, j)
                step(0, 0, 0, False, first=True)

                def body(i):
                    for s in range(2):
                        for j in range(a.nu):
                            if s or j:
                                step(i, s, j, False)
                    step(i + 1, 0, 0, False)
                run_loop(pe, 0, a.pairs - 1, body)
                i = a.pairs - 1
                for s in range(2):
                    for j in range(a.nu):
                        if s or j:
                            step(i, s, j, True)
                pv_of(a.heads - 1, 1, a.nu - 1, True)

            def out_projection(layer):
                name = f"out{layer}"
                u, ev = base(name, "w"), base(name, "ev")
                tiles = range(ROWT[layer])
                pe.wait_ge(o_lo, OL0 + base(name, "hd"))
                for half in range(2):
                    for n in range(2):
                        weights(u)
                        unit_mm(u % 2, tiles, 4, 512, (act_hi, act_lo), 4 * n, n == 0, n == 1)
                        u += 1
                    for b in tiles:
                        last_use[b] = ev + b + 1
                    ev += len(tiles)

            def feed_up(layer):
                name = f"up{layer}"
                F0, U0, full = base(name, "f"), base(name, "w"), layer == 0
                pe.wait_ge(t_free, base(name, "t"))
                pe.wait_ge(acc_evac, base(name, "ev"))
                if full:
                    for k in range(2):
                        ada_mm(ADA_UNITS // 2 + 1, ada_round(1, k), k)

                def product(half, slot):
                    b = 3 * slot
                    wh = w_hi[:, slot, half * 1024:(half + 1) * 1024].rearrange("p (k c) -> p k c", k=KC)
                    wl = w_lo[:, slot, half * 1024:(half + 1) * 1024].rearrange("p (k c) -> p k c", k=KC)
                    regions = [(bank(b + 2 * half), slice(0, LAT))]
                    if full:
                        regions.append((bank(b + 1, CTX, CTX * half), slice(LAT, ROWS)))
                    for k in range(KC):
                        for wt, m, st, sp_ in ((wh, act_hi, k == 0, False), (wh, act_lo, False, False),
                                               (wl, act_hi, False, k == KC - 1)):
                            for o, rows in regions:
                                last = mm(o, wt[:, k, :], m[:, k, rows], start=st, stop=sp_)
                    last.then_inc(mm_done, 1)

                def tile(i, k, free):
                    pe.wait_ge(w_lo_done, i * 2 + (U0 + k + 1))
                    if free:
                        pe.wait_ge(gated, i * 2 + (F0 + k - 1))
                    product(0, k)
                    product(1, k)
                    if full:
                        ada_mm(i + (ADA_UNITS // 2 + 2), i * 2 + (base(name, "t") + 2 + k), k)

                for k in range(2):
                    tile(0, k, False)
                run_loop(pe, 1, FT // 2, lambda i: [tile(i, k, True) for k in range(2)])

            def feed_down(layer):
                name = f"down{layer}"
                U0, G0, ev = base(name, "w"), base(name, "g"), base(name, "ev")
                tiles = range(ROWT[layer])
                pe.wait_ge(gated, base(name, "f"))
                H = FT // 2
                for half in range(2):
                    def unit(i, k, start=False, stop=False):
                        n = half * H + 1 + k
                        pe.wait_ge(w_lo_done, i * 2 + (U0 + n + 1))
                        pe.wait_ge(g_lo, i * 2 + (G0 + n + 1))
                        s = n % 2
                        unit_mm(s, tiles, 2, 512, (act_hi, act_lo), 2 * s, start, stop)
                    unit(0, -1, start=True)
                    run_loop(pe, 0, (H - 3) // 2, lambda i: [unit(i, k) for k in range(2)])
                    unit((H - 3) // 2, 0)
                    unit((H - 3) // 2, 1, stop=True)
                    for b in tiles:
                        last_use[b] = ev + b + 1
                    ev += len(tiles)

            pe.wait_ge(const_in, CONST_IN)
            pe.wait_ge(sc_ready, 1)
            mm(bank(0, 2)[0:2, :], silu[:, 0, :], silu[:, 0, :], start=True, stop=True).then_inc(pv_done, 1)
            for g in range(ADA_FIRST):
                ada_mm(g // 2 + 1, g, g % 2)
            norm_turns("norm0")
            in_projection(0)
            attention("mla", MLA)
            attention("swa", SWA)
            out_projection(0)
            norm_turns("norm1")
            feed_up(0)
            feed_down(0)
            norm_turns("norm2")
            in_projection(1)
            attention("na", NA)
            attention("gqa", GQA)
            out_projection(1)
            norm_turns("norm3")
            feed_up(1)
            feed_down(1)

        @block.scalar
        def _(act):
            A = nc.scalar.activation
            own = Chain(act, act_self)

            for dst, src in CONSTS:
                act.dma_start(dst, src, allow_slow_non_contiguous=True).then_inc(const_in, 16)
            act.wait_ge(const_in, CONST_IN)
            A(cexp[:, :, :], cvec[:, :, :], ACT.Exp, scale=-1.0).then_inc(act_self, 1)
            own.n += 1

            def split_hi(u, s, n, per=None):
                A(w_hi[:, s, 0:n], w_raw[:, s, 0:n], ACT.Copy).then_inc(w_hi_done, 1)

            def w_loaded(u):
                act.wait_ge(w_in[u % 2], 32 * (u // 2 + 1))

            def norm(name):
                y, h = NORMS[name][0] is not None, NORMS[name][1] is not None
                T = NORM_TILES[name]
                squared = []

                def square(src, sum_, sem_, count):
                    n = len(squared)
                    if n >= 2:
                        act.wait_ge(*squared[n - 2])
                    squared.append((sem_, count))
                    A(kilo(12 + n % 2), src, ACT.Square, accum_out=sum_).then_inc(sem_, 1)
                for t in range(T + 2):
                    if y and t < T:
                        if t == 0:
                            act.wait_ge(acc_evac, base(name, "ev"))
                        square(Y[:, t, :], ssy[:, t:t + 1], sum_y, base(name, "y") + t + 1)
                    if h and 1 <= t <= T:
                        q = t - 1
                        if y:
                            act.wait_ge(x_added, base(name, "y") + q + 1)
                            src = x_new[q % 2]
                        else:
                            act.wait_ge(x_ld[q % 2], 16 * (base(name, "xl") // 2 + q // 2 + 1))
                            src = x_in[q % 2]
                        square(src, ssx[:, q:q + 1], sum_x, base(name, "h") + q + 1)
                    if h and t >= 2:
                        q = t - 2
                        for half in range(2):
                            r = base(name, "t") + 2 * q + half
                            act.wait_ge(t_done, r + 1)
                            A(act_hi[:, 4 * half:4 * half + 4, q * P:(q + 1) * P],
                              bank(6 + r % 2).rearrange("p (k r) -> p k r", k=4), ACT.Copy).then_inc(t_hi, 1)

            def projection_splits(units, u0, mm0, tiles_of, between=None):
                done = mm0
                for n, size in enumerate(units):
                    if between is not None:
                        between(n)
                    done += tiles_of[n]
                    if size is None:
                        continue
                    act.wait_ge(mm_done, done)
                    w_loaded(u0 + n + 2)
                    split_hi(u0 + n + 2, (u0 + n) % 2, size)

            def latents(n):
                if n != 4:
                    return
                for b in range(NT):
                    r = base("in0", "t") + 8 + b
                    act.wait_ge(t_done, r + 1)
                    A(lat_t[0][:, :, b * P:(b + 1) * P],
                      bank(6 + r % 2, 3 * P).rearrange("p (k r) -> p k r", k=3), ACT.Copy).then_inc(t_hi, 1)

            def attention(name, a):
                T0, S0, H0 = base(name, "t"), base(name, "s"), base(name, "hd")
                d, dv = a.d, a.dv

                def prep(h, hs, s, rounds):
                    for n in rounds:
                        dst = (qt, kt)[n // 2][s][0]
                        tiles = (a.q_rounds, a.k_rounds)[n // 2][n % 2]
                        act.wait_ge(t_done, a.prep_round(h, n) + (T0 + 1))
                        b = 6 + (T0 + a.prep_round(hs, n)) % 2
                        A(dst[0:d, tiles[0] * P:(tiles[-1] + 1) * P], bank(b, len(tiles) * P)[0:d, :], ACT.Copy)\
                            .then_inc(t_hi, 1)

                def probs_hi(h, j, last_head):
                    at = 0
                    for n, chunks in enumerate(a.units[j][3]):
                        act.wait_ge(t_done, a.unit_round(h, j, last_head) + (T0 + n + 1))
                        b = 6 + (T0 + a.unit_round(0, j, last_head) + n) % 2
                        A(pt[j % 2][0][:, at:at + len(chunks), :],
                          bank(b, len(chunks) * P).rearrange("p (k r) -> p k r", r=P), ACT.Copy).then_inc(t_hi, 1)
                        at += len(chunks)

                def exps(h, j, unit):
                    t, lo, n, _ = a.units[j]
                    p, sb0 = j % 2, (j % 2) * 2
                    wait_apart(act, (mx_done, unit + 1))
                    bias = nb[:, p:p + 1]
                    if a.sink:
                        A(es[:, p:p + 1], sinks[:, ds(h, 1)], ACT.Exp, bias=bias)
                    if a.bias and n:
                        A(prob[p][:, 0:n * P], biased[p][:, 0:n * P], ACT.Exp, bias=bias, scale=a.scale,
                          accum_out=ex[:, p, 0:1])
                        A(prob[p][:, LAT:ROWS], bank(sb0 + 1, CTX), ACT.Exp, bias=bias, scale=a.scale,
                          accum_out=ex[:, p, 1:2]).then_inc(exp_done, 1)
                    else:
                        c = 0 if n else LAT
                        A(prob[p][:, c:ROWS], ps[:, sb0 * 512 + c:sb0 * 512 + ROWS], ACT.Exp, bias=bias,
                          scale=a.scale, accum_out=ex[:, p, 0:1]).then_inc(exp_done, 1)

                def outputs(h, i, s):
                    b = 4 if a.full else 4 + s
                    off = (s * dv) % P
                    wait_apart(act, (pv_done, (h + 1) * a.nu + (S0 + PV0)))
                    k = i + a.mix_chunk if dv == 64 else h + a.mix_chunk
                    A(act_hi[off:off + dv, ds(k, 1), 0:a.acols].rearrange("p o r -> p (o r)"),
                      ps[0:dv, b * 512:b * 512 + a.acols], ACT.Copy).then_inc(o_hi, 1)

                def step(i, s, j, last_pair):
                    h = i * 2 + s
                    last_head = last_pair and s == 1
                    unit = h * a.nu + (S0 + j)
                    at_least(act, pv_done, unit + (PV0 - 1))
                    probs_hi(h, j, last_head)
                    j2, h2 = (j + 2, h) if j + 2 < a.nu else (j + 2 - a.nu, h + 1)
                    if not (last_head and j + 2 >= a.nu):
                        exps(h2, j2, unit + 2)
                    if j == 0 and not (isinstance(h, int) and h == 0):
                        outputs(h - 1, i - 1 if s == 0 else i, 1 - s)
                    if j < 2 and not last_head:
                        prep(h + 1, 2 + (1 - s), 1 - s, (2 * j, 2 * j + 1))

                prep(0, 0, 0, range(4))
                for j in range(2):
                    exps(0, j, S0 + j)
                step(0, 0, 0, False)

                def body(i):
                    for s in range(2):
                        for j in range(a.nu):
                            if s or j:
                                step(i, s, j, False)
                    step(i + 1, 0, 0, False)
                run_loop(act, 0, a.pairs - 1, body)
                i = a.pairs - 1
                for s in range(2):
                    for j in range(a.nu):
                        if s or j:
                            step(i, s, j, True)
                outputs(a.heads - 1, i, 1)

            def half_outs(name, layer, units_left, u0, last_sizes):
                T = ROWT[layer]
                mm0 = base(name, "mm")
                for n in range(4):
                    if n % 2:
                        for t in range(T):
                            act.wait_ge(mm_done, mm0 + n * T + t + 1)
                            A(Y[:, t, (n // 2) * 512:(n // 2 + 1) * 512], bank(t), ACT.Copy).then_inc(acc_evac, 1)
                    act.wait_ge(mm_done, mm0 + (n + 1) * T)
                    w_loaded(u0 + n + 2)
                    split_hi(None, n % 2, 2048)

            def feed_up(layer):
                name = f"up{layer}"
                M0, U0, F0 = base(name, "mm"), base(name, "w"), base(name, "f")
                cols = ROWS if layer == 0 else LAT
                act.wait_ge(x_added, base(name, "y"))

                def tile(i, k, size, free):
                    wait_apart(act, (mm_done, i * 4 + (M0 + 2 * k + (2 if layer == 0 else 1))),
                               *([(gated, i * 2 + (F0 + k - 1))] if free else []))
                    c = conv_acc[:, k, 0:cols]
                    prm = conv[:, layer, ds(i * 2 + k, 1), :]
                    A(c, ps[:, 3 * k * 512:3 * k * 512 + cols], ACT.Identity,
                      scale=prm[:, 0, 1:2], bias=prm[:, 0, 3:4]).then_inc(centre, 1)
                    act.wait_ge(taps, i * 2 + (F0 + k + 1))
                    A(c, c, ACT.Gelu_apprx_tanh).then_inc(gelu, 1)
                    act.wait_ge(mm_done, i * 4 + (M0 + 2 * k + 2))
                    act.wait_ge(w_in[k], i * 32 + (32 * (U0 // 2) + 64))
                    split_hi(None, k, size)

                for k in range(2):
                    tile(0, k, 2048, False)
                run_loop(act, 1, FT // 2 - 1, lambda i: [tile(i, k, 2048, True) for k in range(2)])
                for k in range(2):
                    tile(FT // 2 - 1, k, 1024, True)

            def feed_down(layer, after):
                name = f"down{layer}"
                T, cols = ROWT[layer], (ROWS if layer == 0 else LAT)
                M0, U0, G0, W0 = base(name, "mm"), base(name, "w"), base(name, "g"), base(name, "w")
                H = FT // 2

                def g_split(chunk, s):
                    A(act_hi[:, 2 * s:2 * s + 2, 0:cols], G[:, ds(chunk, 2), 0:cols], ACT.Copy).then_inc(g_hi, 1)

                act.wait_ge(mm_done, M0)
                act.wait_ge(gated, base(name, "f"))
                for n in range(2):
                    g_split(2 * n, n)

                def step(i, k, half, c, w=1024, g=True):
                    n = c + k
                    done = (mm_done, i * (2 * T) + (M0 + (n + 1) * T))
                    if w:
                        wait_apart(act, done, (w_in[n % 2], i * 32 + 32 * ((U0 + n + 2) // 2 + 1)))
                        split_hi(None, n % 2, w)
                    else:
                        wait_apart(act, done)
                    if g:
                        m = n + 2 - (H if n + 2 >= H and half is None else 0)
                        g_split(i * 4 + 2 * ((n + 2) % H if half is None else n + 2 - half * H), n % 2)

                run_loop(act, 0, 4, lambda i: [step(i, k, 0, 0) for k in range(2)])
                step(0, 0, 0, 8)
                step(0, 0, None, 9)
                for t in range(T):
                    act.wait_ge(mm_done, M0 + 10 * T + t + 1)
                    A(Y[:, t, 0:512], bank(t), ACT.Copy).then_inc(acc_evac, 1)
                step(0, 0, None, 10)
                run_loop(act, 0, 4, lambda i: [step(i, k, 1, 11) for k in range(2)])
                step(0, 0, 1, 19)
                step(0, 0, 1, 20, w=after[0], g=False)
                for t in range(T):
                    act.wait_ge(mm_done, M0 + 21 * T + t + 1)
                    A(Y[:, t, 512:1024], bank(t), ACT.Copy).then_inc(acc_evac, 1)
                step(0, 0, 1, 21, w=after[1], g=False)

            for u in range(2):
                w_loaded(u)
                split_hi(u, u, 4 * MLA_IN)
            norm("norm0")
            sizes = [4 * 512] * 2 + [4 * 256] * 2 + [2 * 8 * MLA_D, 16 * NOPE] + [2048] * 2
            projection_splits(sizes, 0, 0, [NT] * 6 + [2 * NT] * 2, latents)
            attention("mla", MLA)
            attention("swa", SWA)
            half_outs("out0", 0, None, base("out0", "w"), None)
            norm("norm1")
            feed_up(0)
            feed_down(0, (2048, 2048))
            norm("norm2")
            tiles = [len(c[2]) for c in IN_CHUNKS[1] for _ in range(2)]
            projection_splits([2048] * 10, base("in1", "w"), base("in1", "mm"), tiles)
            attention("na", NA)
            attention("gqa", GQA)
            half_outs("out1", 1, None, base("out1", "w"), None)
            norm("norm3")
            feed_up(1)
            feed_down(1, (None, None))
            norm("norm4")

        @block.vector
        def _(dve):
            V = nc.vector
            own = Chain(dve, dve_self)

            def minus_hi(out_, full, hi, sem_):
                V.tensor_sub(out_, full, hi.bitcast(fp32)).then_inc(sem_, 1)

            def split_lo(u, s, n):
                dve.wait_ge(w_hi_done, u + 1)
                minus_hi(w_lo[:, s, 0:n], w_raw[:, s, 0:n], w_hi[:, s, 0:n], w_lo_done)

            def ada_evac(r, slot, use):
                dve.wait_ge(t_done, r + 1)
                at_least(dve, ada_out[slot], (use - 1) * 16)
                V.tensor_add(ada_row[:, slot, :], bank(6 + slot, ADA_COLS)[0:2, :], ada_bias[:, slot, :])\
                    .then_inc(t_free, 1)

            def norm(name):
                y, h = NORMS[name][0] is not None, NORMS[name][1] is not None
                T, T0, H0, Y0 = NORM_TILES[name], base(name, "t"), base(name, "h"), base(name, "y")
                dve.wait_ge(mod_ready, base(name, "nm") + 1)
                for t in range(T + 2):
                    if y and t < T:
                        dve.wait_ge(rs_y, Y0 + t + 1)
                        V.scalar_tensor_tensor(out=Y[:, t, :], in0=Y[:, t, :], scalar=rsy[:, t:t + 1],
                                               in1=mod_row[0][t // LT], op0=ALU.mult, op1=ALU.mult)\
                            .then_inc(y_scaled, 1)
                    if h and 1 <= t <= T:
                        q = t - 1
                        dve.wait_ge(rs_x, H0 + q + 1)
                        if q >= 2:
                            dve.wait_ge(t_done, T0 + 2 * (q - 2) + 2)
                        src = x_new[q % 2] if y else x_in[q % 2]
                        V.scalar_tensor_tensor(out=h_tok[q % 2], in0=src, scalar=rsx[:, q:q + 1],
                                               in1=mod_row[1][q // LT], op0=ALU.mult, op1=ALU.mult)\
                            .then_inc(h_scaled, 1)
                    if h and t >= 2:
                        q = t - 2
                        for half in range(2):
                            r = T0 + 2 * q + half
                            dve.wait_ge(t_hi, base(name, "th") + 2 * q + half + 1)
                            cols = (slice(None), slice(4 * half, 4 * half + 4), slice(q * P, (q + 1) * P))
                            minus_hi(act_lo[cols], bank(6 + r % 2).rearrange("p (k r) -> p k r", k=4),
                                     act_hi[cols], t_free)

            def apply_rope(view, tile, w, sem_):
                nh = view.shape[1]
                x = view.rearrange("p h (s w) -> p h s w", s=2)
                a, b = (t[:, 0:nh * 2 * w].rearrange("p (h s w) -> p h s w", h=nh, s=2) for t in tmp)
                cos, sin = (rope[w][:, tile, n, :].unsqueeze(1).unsqueeze(1).to_broadcast([P, nh, 2, w])
                            for n in range(2))
                own.inc(V.tensor_mul(a, x, cos))
                own.inc(V.tensor_mul(b, x, sin))
                own.wait()
                own.inc(V.tensor_sub(x[:, :, 0, :], a[:, :, 0, :], b[:, :, 1, :]))
                last = V.tensor_add(x[:, :, 1, :], a[:, :, 1, :], b[:, :, 0, :])
                if sem_ is None:
                    own.inc(last)
                else:
                    own.wait()
                    last.then_inc(sem_, 1)

            mm_seen, staged_q, ev_norm = [0], [0], [0]

            def chunk(name, tiles, n, norms, gains, ropes, latent=False):
                tiles = list(tiles)
                slots = []

                def evac(x, t):
                    dve.wait_ge(mm_done, mm_seen[0] + x + 1)
                    if latent:
                        dst = mla_in[t]
                    else:
                        s = staged_q[0] % 4
                        at_least(dve, stage_out[s], 16 * (staged_q[0] // 4))
                        dst = stage[s][:, 0:n]
                        staged_q[0] += 1
                    slots.append(dst)
                    last = V.tensor_copy(dst, bank(x, n))
                    last.then_inc(acc_evac, 1)
                    evacs[0] += 1
                    if norms:
                        p = ev_norm[0] % 2
                        if ev_norm[0] >= 2:
                            dve.wait_ge(head_rs, ev_norm[0] - 1)
                        ev_norm[0] += 1
                        dve.wait_ge(acc_evac, evacs[0])
                        for k, (c, w) in enumerate(norms):
                            ins = V.tensor_tensor_reduce(out=tmp[k % 2][:, 0:w], in0=dst[:, c:c + w],
                                                         in1=dst[:, c:c + w], scale=1.0, scalar=0.0,
                                                         op0=ALU.mult, op1=ALU.add,
                                                         accum_out=ssh[:, p, k:k + 1])
                            if k < len(norms) - 1:
                                own.inc(ins)
                                own.wait()
                        ins.then_inc(squares, 1)

                def finish(x, t):
                    dst = slots[x]
                    rp = [r for r in ropes if t < LT]
                    if norms:
                        k0 = ev_norm[0] - (len(slots) - x)
                        dve.wait_ge(head_rs, k0 + 1)
                        p = k0 % 2
                        for k, (c, w) in enumerate(norms):
                            ins = V.scalar_tensor_tensor(out=dst[:, c:c + w], in0=dst[:, c:c + w],
                                                         scalar=rsh[:, p, k:k + 1], in1=gains[k],
                                                         op0=ALU.mult, op1=ALU.mult)
                            own.inc(ins)
                        own.wait()
                    else:
                        dve.wait_ge(acc_evac, evacs[0] - (len(slots) - 1 - x))
                    for k, (view, w) in enumerate(rp):
                        apply_rope(view(dst), t, w, None)
                    if norms or rp:
                        own.wait()

                for x, t in enumerate(tiles):
                    evac(x, t)
                    if norms and x:
                        finish(x - 1, tiles[x - 1])
                        mark()
                    if not norms:
                        finish(x, t)
                        mark()
                if norms:
                    finish(len(tiles) - 1, tiles[-1])
                    mark()
                mm_seen[0] += len(tiles)

            evacs = [0]

            def mark():
                V.tensor_copy(flag[:, 0:1], mhalf[:, 0:1]).then_inc(staged, 1)

            def in_projection(layer):
                name = f"in{layer}"
                W0 = base(name, "w")
                evacs[0] = base(name, "ev")
                mm_seen[0] = base(name, "mm")
                staged_q[0] = base(name, "st")

                def heads_of(c, nh, d, a=0, b=None):
                    return lambda v: v[:, c:c + nh * d].rearrange("p (h d) -> p h d", d=d)[:, :, a:b]
                if layer == 0:
                    todo = [
                        dict(n=MLA_IN, norms=[(0, Q_RANK), (Q_RANK, KV_RANK)],
                             gains=[g_mla[:, 0:Q_RANK], g_mla[:, Q_RANK:]],
                             ropes=[(heads_of(Q_RANK + KV_RANK, 1, ROPE_D), 16)], latent=True),
                        dict(n=512, norms=[], gains=[], ropes=[(heads_of(0, 8, 64), 32)]),
                        dict(n=256, norms=[], gains=[], ropes=[(heads_of(0, 2, 64), 32)]),
                    ]
                    sizes = [2048] * 2 + [1024] * 2 + [2 * 8 * MLA_D, 16 * NOPE] + [2048] * 2
                else:
                    todo = [dict(n=512, norms=[], gains=[], ropes=[])] * 3 + [
                        dict(n=512, norms=[(k * P, P) for k in range(4)], gains=[g_gqa[:, 0, :]] * 4,
                             ropes=[(heads_of(0, 4, P), 64)]),
                        dict(n=512, norms=[(k * P, P) for k in range(2)], gains=[g_gqa[:, 1, :]] * 2,
                             ropes=[(heads_of(0, 2, P), 64)]),
                    ]
                    sizes = [2048] * 10
                n = 0

                def splits_and_ada():
                    split_lo(W0 + n + 2, n % 2, sizes[n])
                    if layer == 0:
                        for k in range(2):
                            g = ADA_FIRST + 2 * n + k
                            ada_evac(ada_round(0, g), k, g // 2 + 1)
                for spec, (_, _, tiles) in zip(todo, IN_CHUNKS[layer]):
                    mm_seen[0] += len(tiles)
                    if layer == 0 and n == 4:
                        for b in range(NT):
                            dve.wait_ge(t_hi, base("in0", "th") + b + 1)
                            r = base("in0", "t") + 8 + b
                            rows = slice(b * P, (b + 1) * P)
                            minus_hi(lat_t[1][:, :, rows], bank(6 + r % 2, 3 * P).rearrange("p (k r) -> p k r", k=3),
                                     lat_t[0][:, :, rows], t_free)
                    splits_and_ada()
                    n += 1
                    chunk(name, tiles, **spec)
                    splits_and_ada()
                    n += 1
                if layer == 0:
                    for kn, cols, ropes in ((2, 384, [(heads_of(0, 4, MLA_D, NOPE, MLA_D), 16)]), (1, 512, [])):
                        for half in range(2):
                            chunk(name, range(NT), cols, [], [], ropes)
                        splits_and_ada()
                        n += 1

            def attention(name, a):
                T0, TH0, S0, H0 = (base(name, k) for k in ("t", "th", "s", "hd"))
                d, dv = a.d, a.dv
                dT = TH0 - T0

                def prep(h, hs, s, rounds):
                    for n in rounds:
                        hi, lo = (qt, kt)[n // 2][s]
                        tiles = (a.q_rounds, a.k_rounds)[n // 2][n % 2]
                        dve.wait_ge(t_hi, a.prep_round(h, n) + (TH0 + 1))
                        b = 6 + (T0 + a.prep_round(hs, n)) % 2
                        cols = slice(tiles[0] * P, (tiles[-1] + 1) * P)
                        minus_hi(lo[0:d, cols], bank(b, len(tiles) * P)[0:d, :], hi[0:d, cols], t_free)

                def probs_lo(h, j, last_head):
                    at = 0
                    for n, chunks in enumerate(a.units[j][3]):
                        dve.wait_ge(t_hi, a.unit_round(h, j, last_head) + (TH0 + n + 1))
                        b = 6 + (T0 + a.unit_round(0, j, last_head) + n) % 2
                        sl = (slice(None), slice(at, at + len(chunks)), slice(None))
                        minus_hi(pt[j % 2][1][sl], bank(b, len(chunks) * P).rearrange("p (k r) -> p k r", r=P),
                                 pt[j % 2][0][sl], t_free)
                        at += len(chunks)

                def maxima(h, s, j, unit):
                    t, lo, n, _ = a.units[j]
                    p, sb0 = j % 2, (j % 2) * 2
                    wait_apart(dve, (s_done, unit + 1),
                               *([(bias_ready, h + 1)] if a.bias == "na" and n else []))
                    m0, m1 = mx[:, p, 0:1], mx[:, p, 1:2]
                    if a.bias and n:
                        if a.bias == "na":
                            bias = na_bias[s][:, (6 - 2 * t) * GRID_W:(6 - 2 * t) * GRID_W + LAT]
                        else:
                            bias = band[:, (lo - t + 1) * P:(lo - t + 1 + n) * P]
                        V.tensor_tensor_reduce(out=biased[p][:, 0:n * P], in0=bank(sb0, n * P), in1=bias,
                                               scale=1.0, scalar=-3.4e38, op0=ALU.add, op1=ALU.max, accum_out=m0)
                        own.inc(V.reduce_max(m1, bank(sb0 + 1, CTX), AX.X))
                        own.wait()
                    else:
                        c = 0 if n else LAT
                        own.inc(V.reduce_max(m0, ps[:, sb0 * 512 + c:sb0 * 512 + ROWS], AX.X))
                        own.wait()
                    second = m1 if a.bias and n else m0
                    if a.sink:
                        own.inc(V.scalar_tensor_tensor(out=m0, in0=m0, scalar=second, in1=sinks8[:, ds(h, 1)],
                                                       op0=ALU.max, op1=ALU.max))
                        own.wait()
                        second = m0
                    V.tensor_scalar(nb[:, p:p + 1], m0, second, -a.scale, ALU.max, ALU.mult).then_inc(mx_done, 1)

                def sums(j, unit):
                    n, p = a.units[j][2], j % 2
                    dve.wait_ge(exp_done, unit + 1)
                    src = ex[:, p, 0:1]
                    if a.bias and n:
                        own.inc(V.tensor_add(rsum[:, p:p + 1], src, ex[:, p, 1:2]))
                        own.wait()
                        src = rsum[:, p:p + 1]
                    if a.sink:
                        own.inc(V.tensor_add(rsum[:, p:p + 1], src, es[:, p:p + 1]))
                        own.wait()
                        src = rsum[:, p:p + 1]
                    V.reciprocal(rinv[:, p:p + 1], src).then_inc(rc_done, 1)

                def outputs(h, i, s):
                    b = 4 if a.full else 4 + s
                    off = (s * dv) % P
                    dve.wait_ge(o_hi, h + (H0 + 1))
                    k = i + a.mix_chunk if dv == 64 else h + a.mix_chunk
                    sl = (slice(off, off + dv), ds(k, 1), slice(0, a.acols))
                    minus_hi(act_lo[sl].rearrange("p o r -> p (o r)"), ps[0:dv, b * 512:b * 512 + a.acols],
                             act_hi[sl].rearrange("p o r -> p (o r)"), o_lo)

                def step(i, s, j, last_pair):
                    h = i * 2 + s
                    last_head = last_pair and s == 1
                    unit = h * a.nu + (S0 + j)
                    j2, s2, h2 = (j + 2, s, h) if j + 2 < a.nu else (j + 2 - a.nu, 1 - s, h + 1)
                    ahead = not (last_head and j + 2 >= a.nu)
                    if ahead:
                        maxima(h2, s2, j2, unit + 2)
                    probs_lo(h, j, last_head)
                    if ahead:
                        sums(j2, unit + 2)
                    if j == 0 and not (isinstance(h, int) and h == 0):
                        outputs(h - 1, i - 1 if s == 0 else i, 1 - s)
                    if j < 2 and not last_head:
                        prep(h + 1, 2 + (1 - s), 1 - s, (2 * j, 2 * j + 1))

                prep(0, 0, 0, range(4))
                for j in range(2):
                    maxima(0, 0, j, S0 + j)
                    sums(j, S0 + j)
                step(0, 0, 0, False)
                grow = 0
                for u in a.units:
                    biased_unit = bool(a.bias and u[2])
                    grow += 1 + (1 if a.sink else 0) + (1 if biased_unit else 0) + (1 if a.sink else 0)

                def body(i):
                    for s in range(2):
                        for j in range(a.nu):
                            if s or j:
                                step(i, s, j, False)
                    step(i + 1, 0, 0, False)
                run_loop(dve, 0, a.pairs - 1, body, own, 2 * grow)
                i = a.pairs - 1
                for s in range(2):
                    for j in range(a.nu):
                        if s or j:
                            step(i, s, j, True)
                outputs(a.heads - 1, i, 1)

            def out_projection(layer):
                for n in range(4):
                    split_lo(base(f"out{layer}", "w") + n + 2, n % 2, 2048)

            def feed_up(layer):
                name = f"up{layer}"
                M0, U0, F0, T0 = (base(name, k) for k in ("mm", "w", "f", "t"))
                full = layer == 0
                cols = ROWS if full else LAT
                for s in range(2):
                    dve.wait_ge(x_st[s], 16 * base(name, "xs") // 2)
                if full:
                    for k in range(2):
                        ada_evac(ada_round(1, k), k, ADA_UNITS // 2 + 1)

                def tile(i, k, size):
                    prm = conv[:, layer, ds(i * 2 + k, 1), :]
                    c, g = conv_acc[:, k, :], ps[:, 3 * k * 512:3 * k * 512 + cols]
                    segments = [(0, LAT)] + ([(LAT, ROWS)] if full else [])
                    dve.wait_ge(centre, i * 2 + (F0 + k + 1))
                    for a, b in segments:
                        own.inc(V.scalar_tensor_tensor(out=c[:, a + 1:b], in0=g[:, a:b - 1], scalar=prm[:, 0, 0:1],
                                                       in1=c[:, a + 1:b], op0=ALU.mult, op1=ALU.add))
                    own.wait()
                    for a, b in segments:
                        last = V.scalar_tensor_tensor(out=c[:, a:b - 1], in0=g[:, a + 1:b], scalar=prm[:, 0, 2:3],
                                                      in1=c[:, a:b - 1], op0=ALU.mult, op1=ALU.add)
                    last.then_inc(taps, 1)
                    dve.wait_ge(gelu, i * 2 + (F0 + k + 1))
                    dve.wait_ge(mm_done, i * 4 + (M0 + 2 * k + 2))
                    dst = G[:, ds(i * 2 + k, 1), :].rearrange("p o r -> p (o r)")
                    if full:
                        V.tensor_mul(dst[:, LAT:ROWS], c[:, LAT:ROWS], bank(3 * k + 1, CTX, CTX))
                    V.tensor_mul(dst[:, 0:LAT], c[:, 0:LAT], bank(3 * k + 2)).then_inc(gated, 1)
                    split_lo(i * 2 + (U0 + k + 2), k, size)
                    if full:
                        ada_evac(i * 2 + (T0 + 2 + k), k, i + (ADA_UNITS // 2 + 2))

                run_loop(dve, 0, FT // 2 - 1, lambda i: [tile(i, k, 2048) for k in range(2)], own,
                         4 if full else 2)
                for k in range(2):
                    tile(FT // 2 - 1, k, 1024)

            def feed_down(layer, after):
                name = f"down{layer}"
                cols = ROWS if layer == 0 else LAT
                U0, G0 = base(name, "w"), base(name, "g")
                H = FT // 2

                def g_split(n, chunk_, s):
                    dve.wait_ge(g_hi, n + (G0 + 1))
                    minus_hi(act_lo[:, 2 * s:2 * s + 2, 0:cols], G[:, ds(chunk_, 2), 0:cols],
                             act_hi[:, 2 * s:2 * s + 2, 0:cols], g_lo)

                for n in range(2):
                    g_split(n, 2 * n, n)

                def step(i, k, c, half, w=1024, g=True):
                    n = c + k
                    if w:
                        split_lo(i * 2 + (U0 + n + 2), n % 2, w)
                    if g:
                        g_split(i * 2 + (n + 2), i * 4 + 2 * ((n + 2) % H if half is None else n + 2 - half * H),
                                n % 2)
                run_loop(dve, 0, 4, lambda i: [step(i, k, 0, 0) for k in range(2)])
                step(0, 0, 8, 0)
                step(0, 0, 9, None)
                step(0, 0, 10, None)
                run_loop(dve, 0, 4, lambda i: [step(i, k, 11, 1) for k in range(2)])
                step(0, 0, 19, 1)
                for n in (20, 21):
                    step(0, 0, n, 1, w=after[n - 20], g=False)

            V.memset(mhalf[:, :], -0.5).then_inc(o_lo, 1)
            dve.wait_ge(const_in, CONST_IN)
            dve.wait_ge(act_self, 1)
            own.inc(V.tensor_scalar_add(cexp[:, :, :], cexp[:, :, :], 1.0))
            own.wait()
            own.inc(V.reciprocal(cexp[:, :, :], cexp[:, :, :]))
            own.wait()
            own.inc(V.tensor_scalar(sinks8[:, :], sinks[:, :], 1.0 / SWA.scale, None, ALU.mult))
            V.tensor_mul(silu[:, :, :], cvec[:, :, :], cexp[:, :, :]).then_inc(sc_ready, 1)
            for g in range(ADA_FIRST):
                ada_evac(g, g % 2, g // 2 + 1)
            for u in range(2):
                split_lo(u, u, 4 * MLA_IN)
            norm("norm0")
            in_projection(0)
            attention("mla", MLA)
            attention("swa", SWA)
            out_projection(0)
            norm("norm1")
            feed_up(0)
            feed_down(0, (2048, 2048))
            norm("norm2")
            in_projection(1)
            attention("na", NA)
            attention("gqa", GQA)
            out_projection(1)
            norm("norm3")
            feed_up(1)
            feed_down(1, (None, None))
            norm("norm4")

        @block.gpsimd
        def _(pool):
            Q = nc.gpsimd
            own = Chain(pool, pool_self)

            def ada_store(layer, r, slot, g):
                pool.wait_ge(t_free, r + 1)
                pool.dma_start(mods[layer, :, ds(g * ADA_COLS, ADA_COLS)], ada_row[:, slot, :])\
                    .then_inc(ada_out[slot], 16)

            def root(dst, src, n, sem_):
                own.inc(Q.tensor_scalar(dst, src, 1.0 / n, EPS, ALU.mult, ALU.add))
                own.wait()
                ins = Q.tensor_tensor(dst, dst, mhalf[:, 0:dst.shape[1]], ALU.pow)
                if sem_ is None:
                    own.inc(ins)
                    own.wait()
                else:
                    ins.then_inc(sem_, 1)

            def norm(name):
                gate, scale, _, _, _, _, store = NORMS[name]
                y, h = gate is not None, scale is not None
                T, Y0, H0 = NORM_TILES[name], base(name, "y"), base(name, "h")
                xl, st = base(name, "xl"), base(name, "xs")
                streams = range(NORM_STREAMS[name])
                pool.wait_ge(mod_in, 16 * (base(name, "mod") + len(streams) * (y + 2 * h)))
                pool.wait_ge(gain_in, 16 * (base(name, "gain") + y + h))
                ops = []
                if h:
                    for v in streams:
                        own.inc(Q.tensor_scalar(mod_row[1][v], mod_row[1][v], 1.0, 1.0, ALU.mult, ALU.add))
                    own.wait()
                    ops += [(mod_row[1][v], h_tok[1]) for v in streams]
                if y:
                    ops += [(mod_row[0][v], h_tok[0]) for v in streams]
                for n, (row, gain) in enumerate(ops):
                    ins = Q.tensor_mul(row, row, gain)
                    if n < len(ops) - 1:
                        own.inc(ins)
                        own.wait()
                ins.then_inc(mod_ready, 1)
                for t in range(T + 1):
                    if y and t < T:
                        pool.wait_ge(sum_y, Y0 + t + 1)
                        root(rsy[:, t:t + 1], ssy[:, t:t + 1], D, rs_y)
                    if h and t:
                        q = t - 1
                        pool.wait_ge(sum_x, H0 + q + 1)
                        root(rsx[:, q:q + 1], ssx[:, q:q + 1], D, rs_x)
                    if y and t < T:
                        pool.wait_ge(y_scaled, Y0 + t + 1)
                        pool.wait_ge(x_ld[t % 2], 16 * (xl // 2 + t // 2 + 1))
                        if t >= 2 and h:
                            pool.wait_ge(h_scaled, H0 + t - 1)
                        at_least(pool, x_st[t % 2], 16 * (st // 2 + t // 2))
                        Q.tensor_add(x_new[t % 2], x_in[t % 2], Y[:, t, :]).then_inc(x_added, 1)
                        pool.wait_ge(x_added, Y0 + t + 1)
                        dst = out[0, t * P:(t + 1) * P, :] if store == "out" else xs[store][t * P:(t + 1) * P, :]
                        pool.dma_start(dst, x_new[t % 2]).then_inc(x_st[t % 2], 16)
                    if h and t:
                        q = t - 1
                        pool.wait_ge(h_scaled, H0 + q + 1)
                        Q.tensor_add(h_tok[q % 2], h_tok[q % 2], mod_row[2][q // LT]).then_inc(h_ready, 1)

            def in_projection(layer):
                name = f"in{layer}"
                done, q, nsq = [base_staged[layer]], [base(name, "st")], [base(name, "nsq")]

                def stores(tiles, n, norm_widths, dst, latent=False):
                    tiles = list(tiles)

                    def rs():
                        p = nsq[0] % 2
                        nsq[0] += 1
                        pool.wait_ge(squares, nsq[0])
                        at = 0
                        for k, (w, cnt) in enumerate(norm_widths):
                            last = k == len(norm_widths) - 1
                            root(rsh[:, p, at:at + cnt], ssh[:, p, at:at + cnt], w, head_rs if last else None)
                            at += cnt

                    def store(t):
                        done[0] += 1
                        pool.wait_ge(staged, done[0])
                        if latent:
                            pool.dma_start(proj[0][t * P:(t + 1) * P, Q_RANK + KV_RANK:MLA_IN],
                                           mla_in[t][:, Q_RANK + KV_RANK:MLA_IN]).then_inc(kpe_out, 16)
                        else:
                            s = q[0] % 4
                            q[0] += 1
                            pool.dma_start(dst[0][t * P:(t + 1) * P, dst[1]:dst[1] + n], stage[s][:, 0:n])\
                                .then_inc(stage_out[s], 16)
                    for x, t in enumerate(tiles):
                        if norm_widths:
                            rs()
                            if x:
                                store(tiles[x - 1])
                        else:
                            store(t)
                    if norm_widths:
                        store(tiles[-1])

                def ada(n):
                    if layer == 0:
                        for k in range(2):
                            g = ADA_FIRST + 2 * n + k
                            ada_store(0, ada_round(0, g), k, g)
                n = 0
                widths = [[(Q_RANK, 1), (KV_RANK, 1)], [], []] if layer == 0 else [[], [], [], [(P, 4)], [(P, 2)]]
                for (c, cn, tiles), nw in zip(IN_CHUNKS[layer], widths):
                    ada(n)
                    stores(tiles, cn, nw, (proj[layer], c), latent=layer == 0 and n == 0)
                    ada(n + 1)
                    n += 2
                if layer == 0:
                    for dst, cols in ((mla_q, 384), (mla_kv, 512)):
                        for half in range(2):
                            stores(range(NT), cols, [], (dst, half * cols))
                        ada(n)
                        n += 1

            def attention(name, a):
                S0, H0 = base(name, "s"), base(name, "hd")

                def values(h, s, loaded, used):
                    wait_apart(pool, (head_in[s], loaded), (pv_done, used))
                    v = v_raw[s][:, 0:NT * a.dv].rearrange("p (t c) -> p t c", c=a.dv)
                    hi, lo = (x[:, :, 0:a.dv] for x in vs[s])
                    own.inc(Q.tensor_copy(hi, v))
                    own.wait()
                    Q.tensor_sub(lo, v, hi.bitcast(fp32)).then_inc(v_split, 1)
                    if a.bias == "na":
                        b = na_bias[s].rearrange("p (r c) -> p r c", c=GRID_W)
                        Q.tensor_add(b, b, colmask[:, :].unsqueeze(1).to_broadcast([P, NA_ROWS, GRID_W]))\
                            .then_inc(bias_ready, 1)

                def scale(j, unit):
                    n, p = a.units[j][2], j % 2
                    wait_apart(pool, (rc_done, unit + 1))
                    for lo_, hi_ in ([(0, ROWS)] if n == LT else [(0, n * P), (LAT, ROWS)] if n else [(LAT, ROWS)]):
                        v = prob[p][:, lo_:hi_]
                        last = Q.tensor_scalar(v, v, rinv[:, p:p + 1], 1.0, ALU.mult, ALU.mult)
                    last.then_inc(p_scaled, 1)

                def step(i, s, j, last_pair):
                    h = i * 2 + s
                    last_head = last_pair and s == 1
                    unit = h * a.nu + (S0 + j)
                    if not (last_head and j + 2 >= a.nu):
                        scale((j + 2) % a.nu, unit + 2)
                    if j == 1 and not last_head:
                        fills = head_fills[name][1 - s]
                        values(h + 1, 1 - s, i * a.load_inc + (fills + (1 if s == 0 else 2) * a.load_inc),
                               h * a.nu + (S0 + PV0))

                values(0, 0, head_fills[name][0] + a.load_inc, S0 + PV0)
                for j in range(2):
                    scale(j, S0 + j)
                step(0, 0, 0, False)

                def body(i):
                    for s in range(2):
                        for j in range(a.nu):
                            if s or j:
                                step(i, s, j, False)
                    step(i + 1, 0, 0, False)
                run_loop(pool, 0, a.pairs - 1, body, own, 2)
                i = a.pairs - 1
                for s in range(2):
                    for j in range(a.nu):
                        if s or j:
                            step(i, s, j, True)

            own.inc(Q.memset(rpb[:, :], 0.0))
            own.wait()
            pool.dma_start(rpb[:, 48:48 + 31], I["na_rpb"][0].rearrange("h r c -> (h r) c")).then_inc(tz_in, 16)
            pool.wait_ge(tz_in, 16)
            own.inc(Q.tensor_scalar(rpb[:, :], rpb[:, :], 1.0 / NA.scale, 1.0, ALU.mult, ALU.mult))
            own.wait()
            pool.dma_start(toeplitz[:, :].rearrange("r (c x) -> r c x", x=TZ_W),
                           rpb[:, 0:TZ_W].unsqueeze(1).to_broadcast([8 * 15, GRID_W, TZ_W])).then_inc(tz_out, 16)
            pool.wait_ge(o_lo, 1)
            for g in range(ADA_FIRST):
                ada_store(0, g, g % 2, g)
            norm("norm0")
            in_projection(0)
            attention("mla", MLA)
            attention("swa", SWA)
            norm("norm1")
            T0 = base("up0", "t")
            for g in range(2):
                ada_store(1, T0 + g, g, g)
            run_loop(pool, 0, FT // 2, lambda i: [ada_store(1, i * 2 + (T0 + 2 + k), k, i * 2 + (2 + k))
                                                  for k in range(2)])
            norm("norm2")
            in_projection(1)
            attention("na", NA)
            attention("gqa", GQA)
            norm("norm3")
            norm("norm4")
            for s in range(2):
                pool.wait_ge(x_st[s], 16 * total["xs"] // 2)
                pool.wait_ge(ada_out[s], 16 * ADA_UNITS)


_INS = ["x", "c", "ctx", "c_ctx", "ada_w", "ada_b", "pre_mix_g", "post_mix_g", "pre_ffn_g", "post_ffn_g",
        "ffn_up", "ffn_conv_w", "ffn_conv_b", "ffn_down", "even_w_in", "even_w_out", "mla_q_norm_g",
        "mla_w_uq", "mla_kv_norm_g", "mla_w_ukv", "swa_sink", "odd_w_in", "odd_w_out", "na_rpb",
        "gqa_q_g", "gqa_k_g"]


def shape_constants():
    f32 = np.float32
    tables = {"ident": np.eye(P, dtype=f32)}
    pos = np.arange(LAT)
    for w in (16, 32, 64):
        d = 2 * w
        freqs = f32(10000.0) ** (-np.arange(d // 4, dtype=f32) * f32(4.0) / f32(d))
        rows, cols = (pos // GRID_W).astype(f32), (pos % GRID_W).astype(f32)
        ang = np.concatenate([rows[:, None] * freqs, cols[:, None] * freqs], axis=-1).astype(f32)
        t = np.stack([np.cos(ang), np.sin(ang)], axis=1)
        tables[f"rope{w}"] = np.ascontiguousarray(t.reshape(LT, P, 2, w).transpose(1, 0, 2, 3)).astype(f32)
    q, k = np.arange(P)[:, None], np.arange(P)[None, :]
    zero, neg = f32(0), f32(NEG)
    tables["band"] = np.concatenate([np.where(k >= q, zero, neg), np.zeros((P, P), f32),
                                     np.where(k <= q, zero, neg)], axis=1).astype(f32)
    c = np.arange(P)[:, None] % GRID_W
    start = np.clip(c - 8, 0, GRID_W - 16)
    kc = np.arange(GRID_W)[None, :]
    tables["colmask"] = np.where((kc >= start) & (kc < start + 16), zero, neg).astype(f32)
    return tables


def kernel(**inputs):
    import concourse.bacc as _bacc
    from concourse.bass_utils import run_bass_kernel_spmd as _run

    nc = _bacc.Bacc("TRN2", target_bir_lowering=False, num_devices=1)
    arrays, I, C = {}, {}, {}
    for group, named in ((I, {n: inputs[n] for n in _INS}), (C, shape_constants())):
        for name, a in named.items():
            a = np.ascontiguousarray(a)
            arrays[f"in_{name}"] = a
            group[name] = nc.dram_tensor(f"in_{name}", a.shape, mybir.dt.from_np(a.dtype),
                                         kind="ExternalInput").ap()
    out = nc.dram_tensor("out_0", (1, LAT, D), mybir.dt.float32, kind="ExternalOutput").ap()
    build(nc, I, C, out)
    r = _run(nc, [arrays], core_ids=[0])
    return r.results[0]["out_0"]
```

```python
import math
from contextlib import ExitStack

import concourse.bass as bass
import numpy as np
from concourse import mybir

P = 128
D = 1024
LAT, CTX = 512, 256
ROWS = LAT + CTX
LT, NT = LAT // P, ROWS // P
KC = D // P
GRID_W = 64
EPS = 1e-6
NEG = -1e30
Q_RANK, KV_RANK, ROPE_D, NOPE = 256, 128, 32, 64
MLA_IN = Q_RANK + KV_RANK + ROPE_D
MLA_D = NOPE + ROPE_D
EVEN_IN, ODD_IN = 1184, 2560
FF = 2816
FT = FF // P
ADA_COLS = 256
ADA_UNITS = 6 * D // ADA_COLS
ADA_FIRST = 2 * D // ADA_COLS
TZ_W = 2 * GRID_W - 1
NA_ROWS = 14


class Chain:

    def __init__(self, eng, sem):
        self.eng, self.sem, self.n, self.term = eng, sem, 0, 0

    def inc(self, instruction):
        instruction.then_inc(self.sem, 1)
        self.n += 1

    def wait(self):
        self.eng.wait_ge(self.sem, self.term + self.n)


def run_loop(eng, first, last, body, chain=None, growth=0):
    if last <= first:
        return
    if last == first + 1:
        body(first)
        return
    with eng.Fori(first, last) as i:
        if chain is not None:
            start = chain.n
            chain.term = (i - first) * growth if growth else 0
        body(i)
        if chain is not None:
            assert chain.n - start == growth, (chain.n - start, growth)
            chain.term, chain.n = 0, start + growth * (last - first)


class Attention:

    def __init__(self, name, heads, d, dv, units, mix_chunk, banded=False, bias=None, sink=False):
        self.name, self.heads, self.d, self.dv, self.mix_chunk = name, heads, d, dv, mix_chunk
        self.bias, self.sink = bias, sink
        self.scale = d ** -0.5
        self.nu = units
        self.pairs = heads // 2
        self.full = units == NT
        self.units = []
        for t in range(units):
            if t >= LT:
                lo, n = 0, 0
            elif banded:
                lo = max(t - 1, 0)
                n = min(t + 2, LT) - lo
            else:
                lo, n = 0, LT
            chunks = [(c * P, lo + c) for c in range(n)] + [(LAT + c * P, LT + c) for c in range(NT - LT)]
            if n == 0:
                rounds = [chunks]
            elif banded:
                rounds = [chunks[:n], chunks[n:]]
            else:
                rounds = [chunks[:3], chunks[3:]]
            self.units.append((t, lo, n, rounds))
        self.unit_rounds = [len(u[3]) for u in self.units]
        self.q_rounds = [[0, 1, 2], [3, 4, 5]] if self.full else [[0, 1], [2, 3]]
        self.k_rounds = [[0, 1, 2], [3, 4, 5]]
        self.head_rounds = sum(self.unit_rounds) + 4
        self.total_rounds = 4 + (heads - 1) * self.head_rounds + sum(self.unit_rounds)
        self.load_inc = 16 * {"mla": 4, "swa": 3, "na": 5, "gqa": 3}[name]
        self.acols = ROWS if self.full else LAT
        self.prep_rounds = [(), (0, 1), (2, 3), (), (), ()] if self.full else [(0, 1, 2, 3), (), (), ()]
        assert self.head_rounds % 2 == 0 and self.total_rounds % 2 == 0 and units % 2 == 0

    def _before(self, j, last_head):
        return sum(self.unit_rounds[:j]) + (0 if last_head else sum(map(len, self.prep_rounds[:j])))

    def unit_round(self, h, j, last_head):
        return h * self.head_rounds + (4 + self._before(j, last_head))

    def prep_round(self, h, n):
        if isinstance(h, int) and h == 0:
            return n
        j = next(j for j, rounds in enumerate(self.prep_rounds) if n in rounds)
        return (h - 1) * self.head_rounds + (4 + self._before(j, False) + self.unit_rounds[j] + self.prep_rounds[j].index(n))

    def prep_end(self, h):
        return self.prep_round(h, 3) + 1


def build(nc, I, C, out):
    fp32, f32r = mybir.dt.float32, mybir.dt.float32r
    ALU, ACT, AX = mybir.AluOpType, mybir.ActivationFunctionType, mybir.AxisListType
    ds = bass.ds

    def scratch(name, shape):
        return nc.dram_tensor(name, shape, fp32)

    proj = [scratch("proj_even", [ROWS, EVEN_IN]), scratch("proj_odd", [ROWS, ODD_IN])]
    mla_q = scratch("mla_q", [ROWS, 8 * MLA_D])
    mla_kv = scratch("mla_kv", [ROWS, 8 * 2 * NOPE])
    xs = [scratch(f"x_after_{n}", [ROWS, D]) for n in ("mix0", "ffn0", "mix1")]
    mods = scratch("mods", [2, 2, 6 * D])
    toeplitz = scratch("toeplitz", [8 * 15, GRID_W * TZ_W])

    ctx = ExitStack()
    with ctx:
        def sb(name, shape, dt=fp32):
            return ctx.enter_context(nc.sbuf_tensor(name, shape, dt))

        def sem(name):
            return ctx.enter_context(nc.semaphore(name))

        G_EL, Y_EL = FT * ROWS, NT * D
        arena_at = (nc.sbuf_base + 31) // 32 * 32
        arena = sb("arena", [P, G_EL + Y_EL])
        act_hi, act_lo = sb("act_hi", [P, KC, ROWS], f32r), sb("act_lo", [P, KC, ROWS], f32r)
        w_raw = sb("w_raw", [P, 2, 2048])
        w_hi, w_lo = sb("w_hi", [P, 2, 2048], f32r), sb("w_lo", [P, 2, 2048], f32r)
        ident = sb("ident", [P, P])
        rope = {w: sb(f"rope{w}", [P, LT, 2, w]) for w in (16, 32, 64)}
        band = sb("band", [P, 3 * P])
        colmask = sb("colmask", [P, GRID_W])
        conv = sb("conv", [P, 2, FT, 4])
        cvec, cexp = sb("cvec", [P, KC, 2]), sb("cexp", [P, KC, 2])
        silu = sb("silu", [P, KC, 2])
        stream = sb("stream", [P, 2, 2])
        g_mla = sb("g_mla", [P, Q_RANK + KV_RANK])
        g_gqa = sb("g_gqa", [P, 2, P])
        sinks, sinks8 = sb("sinks", [P, 8]), sb("sinks8", [P, 8])
        ada_bias, ada_row = sb("ada_bias", [2, 2, ADA_COLS]), sb("ada_row", [2, 2, ADA_COLS])
        rpb = sb("rpb", [8 * 15, P])
        flag = sb("flag", [P, 1])
        mhalf = sb("mhalf", [P, 8])
        ssy, ssx = sb("ssy", [P, NT]), sb("ssx", [P, NT])
        rsy, rsx = sb("rsy", [P, NT]), sb("rsx", [P, NT])
        ssh, rsh = sb("ssh", [P, 2, 4]), sb("rsh", [P, 2, 4])
        mx, nb = sb("mx", [P, 2, 2]), sb("nb", [P, 2])
        ex, es = sb("ex", [P, 2, 2]), sb("es", [P, 2])
        rsum, rinv = sb("rsum", [P, 2]), sb("rinv", [P, 2])

        G = arena[:, 0:G_EL].rearrange("p (t r) -> p t r", t=FT)
        Y = arena[:, G_EL:G_EL + Y_EL].rearrange("p (t d) -> p t d", t=NT)
        conv_acc = arena[:, G_EL:G_EL + 2 * ROWS].rearrange("p (s r) -> p s r", s=2)
        ada_raw = arena[:, G_EL + 2 * ROWS:G_EL + 2 * ROWS + 4096].rearrange("p (s k c) -> p s k c", s=2, k=KC)
        ada_sum = arena[:, G_EL + Y_EL - 2 * ADA_COLS:].rearrange("p (v c) -> p v c", v=2)

        def kilo(n):
            return arena[:, n * D:(n + 1) * D]
        mod_row = [[kilo(2 * m + v) for v in range(2)] for m in range(3)]
        x_in = [kilo(6), kilo(7)]
        x_new = [kilo(8), kilo(9)]
        h_tok = [kilo(10), kilo(11)]

        at = [arena_at]

        def split(name, shape):
            n = math.prod(shape[1:])
            t = nc.alloc_sbuf_tensor_at(name, shape, f32r, offset=at[0])
            at[0] += 4 * n
            return t
        c_at = at[0]
        qt = [[split(f"qt_{x}{i}", [P, ROWS]) for x in ("hi", "lo")] for i in range(2)]
        kt = [[split(f"kt_{x}{i}", [P, ROWS]) for x in ("hi", "lo")] for i in range(2)]
        vs = [[split(f"v_{x}{i}", [P, NT, P]) for x in ("hi", "lo")] for i in range(2)]
        pt = [[split(f"pt_{x}{i}", [P, NT, P]) for x in ("hi", "lo")] for i in range(2)]
        at_end = at[0]
        at[0] = c_at
        lat_t = [split(f"latent_{x}", [P, 3, ROWS]) for x in ("hi", "lo")]
        at[0] = at_end
        cur = [(at_end - arena_at) // 4]

        def plain(n):
            v = arena[:, cur[0]:cur[0] + n]
            cur[0] += n
            assert cur[0] <= G_EL + Y_EL
            return v
        plain_at = cur[0]
        q_raw = [plain(NT * P) for _ in range(2)]
        k_raw = [plain(NT * P) for _ in range(2)]
        v_raw = [plain(NT * P) for _ in range(2)]
        prob = [plain(ROWS) for _ in range(2)]
        biased = [plain(LAT) for _ in range(2)]
        na_bias = [plain(NA_ROWS * GRID_W) for _ in range(2)]
        cur[0] = plain_at - 2 * D
        stage = [plain(512) for _ in range(4)]
        mla_in = [plain(MLA_IN) for _ in range(NT)]
        cur[0] = G_EL
        tmp = [plain(512) for _ in range(2)]
        assert cur[0] <= G_EL + 2 * ROWS

        ps = ctx.enter_context(nc.psum_tensor("ps", [P, 8 * 512], fp32))

        def bank(b, n=512, off=0):
            return ps[:, b * 512 + off:b * 512 + off + n]

        c_in, const_in = sem("c_in"), sem("const_in")
        passed = sem("passed")
        sc_ready, ada_summed = sem("sc_ready"), sem("ada_summed")
        w_in = [sem("w_in0"), sem("w_in1")]
        w_hi_done, w_lo_done = sem("w_hi_done"), sem("w_lo_done")
        ada_in = [sem("ada_in0"), sem("ada_in1")]
        ada_out = [sem("ada_out0"), sem("ada_out1")]
        mm_done = sem("mm_done")
        acc_evac = sem("acc_evac")
        t_done, t_hi, t_free = sem("t_done"), sem("t_hi"), sem("t_free")
        mod_in, gain_in = sem("mod_in"), sem("gain_in")
        x_ld = [sem("x_ld0"), sem("x_ld1")]
        x_st = [sem("x_st0"), sem("x_st1")]
        sum_y, rs_y, y_scaled, x_added = sem("sum_y"), sem("rs_y"), sem("y_scaled"), sem("x_added")
        sum_x, rs_x, h_scaled, h_ready = sem("sum_x"), sem("rs_x"), sem("h_scaled"), sem("h_ready")
        squares, head_rs = sem("squares"), sem("head_rs")
        staged = sem("staged")
        stage_out = [sem(f"stage_out{i}") for i in range(4)]
        kpe_out = sem("kpe_out")
        head_in = [sem("head_in0"), sem("head_in1")]
        v_split, bias_ready = sem("v_split"), sem("bias_ready")
        s_done, mx_done, exp_done, rc_done, p_scaled = (sem("s_done"), sem("mx_done"), sem("exp_done"),
                                                        sem("rc_done"), sem("p_scaled"))
        pv_done, o_hi, o_lo = sem("pv_done"), sem("o_hi"), sem("o_lo")
        centre, taps, gelu, gated = sem("centre"), sem("taps"), sem("gelu"), sem("gated")
        g_hi, g_lo = sem("g_hi"), sem("g_lo")
        dve_self, act_self, pool_self = sem("dve_self"), sem("act_self"), sem("pool_self")
        tz_in, tz_out = sem("tz_in"), sem("tz_out")

        block = ctx.enter_context(nc.Block())

        MLA = Attention("mla", 8, MLA_D, 64, NT, 0)
        SWA = Attention("swa", 8, 64, 64, NT, 4, banded=True, bias="band", sink=True)
        NA = Attention("na", 8, 64, 64, LT, 0, bias="na")
        GQA = Attention("gqa", 4, 128, 128, LT, 4)
        ATT = [[MLA, SWA], [NA, GQA]]

        head_fills = {"mla": [0, 0]}
        for prev, a in ((MLA, SWA), (SWA, NA), (NA, GQA)):
            head_fills[a.name] = [n + prev.heads // 2 * prev.load_inc for n in head_fills[prev.name]]

        IN_CHUNKS = [[(0, MLA_IN, range(NT)), (MLA_IN, 512, range(NT)), (MLA_IN + 512, 256, range(NT))],
                     [(0, 512, range(LT)), (512, 512, range(NT)), (1024, 512, range(NT)),
                      (1536, 512, range(LT)), (2048, 512, range(NT))]]
        ROWT = [NT, LT]

        CVEC = [(cvec[:, :, :], C["streams"])]
        CONSTS = [(ident[:, :], C["ident"]), (band[:, :], C["band"]), (colmask[:, :], C["colmask"])]
        CONSTS += [(rope[w][:, :, :, :], C[f"rope{w}"]) for w in rope]
        CONSTS += [(conv[:, :, :, :], C["conv"])]
        CONSTS += [(g_mla[:, 0:Q_RANK], I["mla_q_norm_g"].to_broadcast([P, Q_RANK])),
                   (g_mla[:, Q_RANK:], I["mla_kv_norm_g"].to_broadcast([P, KV_RANK])),
                   (g_gqa[:, 0, :], I["gqa_q_g"].to_broadcast([P, P])),
                   (g_gqa[:, 1, :], I["gqa_k_g"].to_broadcast([P, P])),
                   (sinks[:, :], I["swa_sink"].to_broadcast([P, 8]))]
        CONST_IN = 16 * len(CONSTS)

        def att_growth(a):
            return dict(t=a.total_rounds, th=a.total_rounds, s=a.heads * a.nu, hd=a.heads)

        def norm_growth(tiles, y, h, streams):
            return dict(t=2 * tiles * h, th=2 * tiles * h, y=tiles * y, h=tiles * h, xl=tiles, xs=tiles * y,
                        mod=streams * (y + 2 * h), gain=y + h, nm=1)

        N0, N1 = ROWT
        accs = [sum(len(c[2]) for c in IN_CHUNKS[l]) for l in range(2)]
        PHASES = [
            ("ada", dict(t=ADA_FIRST)),
            ("norm0", norm_growth(NT, 0, 1, 2)),
            ("in0", dict(t=22, th=NT, mm=2 * accs[0] + 4 * NT, w=8, ev=accs[0] + 4 * NT,
                         st=accs[0] - NT + 4 * NT, nsq=NT)),
            ("mla", att_growth(MLA)), ("swa", att_growth(SWA)),
            ("out0", dict(mm=4 * N0, w=4, ev=2 * N0)),
            ("norm1", norm_growth(N0, 1, 1, 2)),
            ("up0", dict(t=ADA_UNITS, mm=2 * FT, w=FT, f=FT)),
            ("down0", dict(mm=FT * N0, w=FT, ev=2 * N0, g=FT)),
            ("norm2", norm_growth(NT, 1, 1, 2)),
            ("in1", dict(mm=2 * accs[1], w=10, ev=accs[1], st=accs[1], nsq=LT + NT)),
            ("na", att_growth(NA)), ("gqa", att_growth(GQA)),
            ("out1", dict(mm=4 * N1, w=4, ev=2 * N1)),
            ("norm3", norm_growth(N1, 1, 1, 1)),
            ("up1", dict(mm=2 * FT, w=FT, f=FT)),
            ("down1", dict(mm=2 * FT // 2 * N1, w=FT, ev=2 * N1, g=FT)),
            ("norm4", norm_growth(N1, 1, 0, 1)),
        ]
        BASE, total = {}, dict.fromkeys("t th mm w ev st s hd y h xl xs mod gain nm nsq f g".split(), 0)
        for name, growth in PHASES:
            BASE[name] = dict(total)
            for k, v in growth.items():
                total[k] += v

        base_staged = [0, accs[0] + 4 * NT]

        def base(name, what):
            return BASE[name][what]

        PV0 = OL0 = 1

        ADA_IN0 = list(range(8)) + list(range(14, 22))

        def ada_round(layer, g):
            if layer == 0:
                return g if g < ADA_FIRST else base("in0", "t") + ADA_IN0[g - ADA_FIRST]
            return base("up0", "t") + g

        def at_least(eng, sem, value):
            if not (isinstance(value, int) and value <= 0):
                eng.wait_ge(sem, value)

        def stages_stored(eng, n):
            for s in range(4):
                eng.wait_ge(stage_out[s], 16 * ((n + 3 - s) // 4))

        def wait_apart(eng, *waits):
            for s, v in waits:
                eng.wait_ge(s, v)
                eng.sem_inc(passed, 1)

        NORMS = {
            "norm0": (None, (0, 1), (0, 0), None, ("pre_mix_g", 0), None, None),
            "norm1": ((0, 2), (0, 4), (0, 3), ("post_mix_g", 0), ("pre_ffn_g", 0), None, 0),
            "norm2": ((0, 5), (1, 1), (1, 0), ("post_ffn_g", 0), ("pre_mix_g", 1), 0, 1),
            "norm3": ((1, 2), (1, 4), (1, 3), ("post_mix_g", 1), ("pre_ffn_g", 1), 1, 2),
            "norm4": ((1, 5), None, None, ("post_ffn_g", 1), None, 2, "out"),
        }
        NORM_TILES = {"norm0": NT, "norm1": N0, "norm2": NT, "norm3": N1, "norm4": N1}
        NORM_STREAMS = {"norm0": 2, "norm1": 2, "norm2": 2, "norm3": 1, "norm4": 1}

        def x_source(name, t):
            k = NORMS[name][5]
            if k is None:
                return I["x"][0, t * P:(t + 1) * P, :] if t < LT else I["ctx"][0, (t - LT) * P:(t - LT + 1) * P, :]
            return xs[k][t * P:(t + 1) * P, :]

        def up_cols(t, half):
            return t * P + half * FF

        @block.sync
        def _(sp):
            def raw_free(u):
                at_least(sp, w_lo_done, u - 1)

            def k_unit(u, w, k0, kn, c0, cn):
                raw_free(u)
                v = w.rearrange("(k p) c -> p k c", p=P)
                dst = w_raw[:, u % 2, 0:kn * cn].rearrange("p (k c) -> p k c", c=cn)
                if kn == 1:
                    for a, b in ((0, cn // 2), (cn // 2, cn)):
                        sp.dma_start(dst[:, 0, a:b], v[:, k0, c0 + a:c0 + b]).then_inc(w_in[u % 2], 16)
                else:
                    for a, b in ((0, kn // 2), (kn // 2, kn)):
                        sp.dma_start(dst[:, a:b, :], v[:, k0 + a:k0 + b, c0:c0 + cn]).then_inc(w_in[u % 2], 16)

            def up_unit(layer, t, slot):
                v = I["ffn_up"][layer].rearrange("(k p) c -> p k c", p=P)
                for half in range(2):
                    dst = w_raw[:, slot, half * 1024:(half + 1) * 1024].rearrange("p (k c) -> p k c", k=KC)
                    sp.dma_start(dst, v[:, :, ds(up_cols(t, half), P)]).then_inc(w_in[slot], 16)

            def down_unit(layer, k, half, slot):
                for j in range(2):
                    src = I["ffn_down"][layer][ds((k + j) * P, P), half * 512:(half + 1) * 512]
                    sp.dma_start(w_raw[:, slot, j * 512:(j + 1) * 512], src).then_inc(w_in[slot], 16)

            def ada_unit(layer, g, slot):
                v = I["ada_w"][layer].rearrange("(k p) c -> p k c", p=P)
                sp.dma_start(ada_raw[:, slot], v[:, :, ds(g * ADA_COLS, ADA_COLS)]).then_inc(ada_in[slot], 16)
                b = I["ada_b"][layer:layer + 1, ds(g * ADA_COLS, ADA_COLS)]
                sp.dma_start(ada_bias[:, slot], b.to_broadcast([2, ADA_COLS])).then_inc(ada_in[slot], 16)

            def mod_loads(name):
                gate, scale, shift = NORMS[name][:3]
                last = {"norm0": 8, "norm1": 24, "norm2": 32, "norm3": 48, "norm4": 48}[name]
                for s in range(2):
                    sp.wait_ge(ada_out[s], 16 * last // 2)
                for m, lc in enumerate((gate, scale, shift)):
                    if lc is None:
                        continue
                    for v in range(NORM_STREAMS[name]):
                        src = mods[lc[0], v:v + 1, lc[1] * D:(lc[1] + 1) * D]
                        sp.dma_start(mod_row[m][v], src.to_broadcast([P, D])).then_inc(mod_in, 16)

            def gain_loads(name):
                post, pre = NORMS[name][3:5]
                for n, g in enumerate((post, pre)):
                    if g is not None:
                        src = I[g[0]][g[1]:g[1] + 1, :]
                        sp.dma_start(h_tok[n], src.to_broadcast([P, D])).then_inc(gain_in, 16)

            def x_moves(name, tiles):
                T, st = NORM_TILES[name], NORMS[name][6]
                for t in tiles:
                    if t < 2 and NORMS[name][5] is not None:
                        for s in range(2):
                            sp.wait_ge(x_st[s], 16 * base(name, "xs") // 2)
                    if t >= 2 and NORMS[name][0] is None:
                        sp.wait_ge(h_scaled, base(name, "h") + t - 1)
                    elif t >= 2:
                        sp.wait_ge(x_added, base(name, "y") + t - 1)
                        q = t - 2
                        dst = out[0, q * P:(q + 1) * P, :] if st == "out" else xs[st][q * P:(q + 1) * P, :]
                        sp.dma_start(dst, x_new[q % 2]).then_inc(x_st[q % 2], 16)
                    if t < T:
                        sp.dma_start(x_in[t % 2], x_source(name, t)).then_inc(x_ld[t % 2], 16)

            def head_loads(name, a, before):
                def rows(src, c, n, tiles=NT):
                    return src[0:tiles * P, ds(c, n)].rearrange("(t p) c -> p t c", p=P)

                def load(h, s):
                    def put(dst, src):
                        sp.dma_start(dst, src).then_inc(head_in[s], 16)
                    q = q_raw[s][:, 0:NT * a.d].rearrange("p (t c) -> p t c", c=a.d)[:, 0:a.nu]
                    k = k_raw[s][:, 0:NT * a.d].rearrange("p (t c) -> p t c", c=a.d)
                    v = v_raw[s][:, 0:NT * a.dv].rearrange("p (t c) -> p t c", c=a.dv)
                    if a.name == "mla":
                        put(q, rows(mla_q, h * MLA_D, MLA_D))
                        put(k[:, :, 0:NOPE], rows(mla_kv, h * 2 * NOPE, NOPE))
                        put(k[:, :, NOPE:MLA_D], rows(proj[0], Q_RANK + KV_RANK, ROPE_D))
                        put(v, rows(mla_kv, h * 2 * NOPE + NOPE, NOPE))
                    elif a.name == "swa":
                        kv = (h // 4) * 64
                        put(q, rows(proj[0], h * 64 + MLA_IN, 64))
                        put(k, rows(proj[0], kv + MLA_IN + 512, 64))
                        put(v, rows(proj[0], kv + MLA_IN + 640, 64))
                    elif a.name == "na":
                        put(q, rows(proj[1], h * 64, 64, LT))
                        put(k, rows(proj[1], h * 64 + 512, 64))
                        put(v, rows(proj[1], h * 64 + 1024, 64))
                        for rl in range(2):
                            src = toeplitz[ds(h * 15 + (1 - rl), NA_ROWS),
                                           GRID_W - 1:GRID_W - 1 + GRID_W * (TZ_W - 1)]\
                                .rearrange("r (c x) -> c r x", x=TZ_W - 1)[:, :, 0:GRID_W]
                            dst = na_bias[s][rl * GRID_W:(rl + 1) * GRID_W, :].rearrange("p (r c) -> p r c", c=GRID_W)
                            put(dst, src)
                    else:
                        put(q, rows(proj[1], h * P + 1536, P, LT))
                        kv = (h // 2) * P
                        put(k, rows(proj[1], kv + 2048, P))
                        put(v, rows(proj[1], kv + 2048 + 256, P))

                for h in range(2):
                    if before is not None:
                        pn, pa = before
                        hp = pa.heads - 2 + h
                        sp.wait_ge(t_free, base(pn, "t") + pa.prep_end(hp))
                        sp.wait_ge(v_split, base(pn, "hd") + hp + 1)
                    load(h, h)

                def pair(i):
                    for s in range(2):
                        h = i * 2 + s
                        waits = [(t_free, a.prep_end(h - 2) + base(name, "t")),
                                 (v_split, h + (base(name, "hd") - 1))]
                        if a.bias == "na":
                            waits.append((mx_done, (h - 1) * a.nu + base(name, "s")))
                        wait_apart(sp, *waits)
                        load(h, s)
                if a.name in ("swa", "gqa"):
                    for i in range(1, a.pairs):
                        pair(i)
                else:
                    pair(1)
                    run_loop(sp, 2, a.pairs, pair)

            for g in range(ADA_FIRST):
                if g >= 2:
                    sp.wait_ge(t_free, ada_round(0, g - 2) + 1)
                ada_unit(0, g, g % 2)
                if g == 2:
                    x_moves("norm0", range(2))
            gain_loads("norm0")
            for n in range(2):
                k_unit(n, I["even_w_in"][0], 4 * n, 4, 0, MLA_IN)
            mod_loads("norm0")
            x_moves("norm0", range(2, NT))
            units = [(I["even_w_in"][0], 4 * n, 4, c, cn) for c, cn, _ in IN_CHUNKS[0] for n in range(2)]
            units += [(I["mla_w_uq"][0], 0, 2, 0, 8 * MLA_D), (I["mla_w_ukv"][0], 0, 1, 0, 16 * NOPE)]
            units += [(I["even_w_out"][0], 4 * n, 4, c, 512) for c in (0, 512) for n in range(2)]
            for n in range(8):
                for g in range(ADA_FIRST + 2 * n, ADA_FIRST + 2 * n + 2):
                    sp.wait_ge(t_free, ada_round(0, g - 2) + 1)
                    ada_unit(0, g, g % 2)
                k_unit(n + 2, *units[n + 2])
            for layer in range(2):
                names = [("mla", "swa"), ("na", "gqa")][layer]
                nm, nf = ("norm1", "norm2") if layer == 0 else ("norm3", "norm4")
                if layer == 0:
                    stages_stored(sp, base("mla", "st"))
                    sp.wait_ge(kpe_out, 16 * NT)
                else:
                    stages_stored(sp, base("in1", "st") + LT + 2 * NT)
                    sp.wait_ge(tz_out, 16)
                head_loads(names[0], ATT[layer][0], None)
                for n in (-2, -1):
                    k_unit(base(f"out{layer}", "w") + 4 + n, *units[n])
                if layer == 1:
                    stages_stored(sp, base("na", "st"))
                head_loads(names[1], ATT[layer][1], (names[0], ATT[layer][0]))
                sp.wait_ge(o_lo, OL0 + base(nm, "hd"))
                mod_loads(nm)
                gain_loads(nm)
                x_moves(nm, range(2))
                up, w_up, w_down = f"up{layer}", base(f"up{layer}", "w"), base(f"down{layer}", "w")
                for t in range(2):
                    raw_free(w_up + t)
                    up_unit(layer, t, t)
                x_moves(nm, range(2, ROWT[layer] + 2))
                if layer == 0:
                    sp.wait_ge(x_added, base(nm, "y") + NT)
                    for g in range(2):
                        ada_unit(1, g, g)

                def up_trip(i):
                    for k in range(2):
                        wait_apart(sp, (w_lo_done, i * 2 + (w_up + 2 + k - 1)))
                        up_unit(layer, i * 2 + (k + 2), k)
                        if layer == 0:
                            wait_apart(sp, (t_free, i * 2 + (base(up, "t") + k + 1)))
                            ada_unit(1, i * 2 + (k + 2), k)
                run_loop(sp, 0, FT // 2 - 1, up_trip)
                for half in range(2):
                    w0 = w_down + half * (FT // 2)

                    def down_trip(i):
                        for k in range(2):
                            wait_apart(sp, (w_lo_done, i * 2 + (w0 + k - 1)))
                            down_unit(layer, i * 4 + 2 * k, half, (w0 + k) % 2)
                    down_trip(0)
                    if layer == half == 0:
                        for k in range(2):
                            sp.wait_ge(t_free, ada_round(1, FT - 2 + k) + 1)
                            ada_unit(1, FT + k, k)
                            run_loop(sp, 1 + 2 * k, 3 + 2 * k, down_trip)
                    else:
                        run_loop(sp, 1, FT // 4, down_trip)
                    sp.wait_ge(w_lo_done, w0 + FT // 2 - 1 - 1)
                    down_unit(layer, 4 * (FT // 4), half, (w0 + FT // 2 - 1) % 2)
                sp.wait_ge(g_lo, base(f"down{layer}", "g") + 16)
                mod_loads(nf)
                if layer == 0:
                    w_in1 = base("in1", "w")
                    units = [(I["odd_w_in"][0], 4 * n, 4, c, cn) for c, cn, _ in IN_CHUNKS[1] for n in range(2)]
                    units += [(I["odd_w_out"][0], 4 * n, 4, c, 512) for c in (0, 512) for n in range(2)]
                    for n in range(2):
                        k_unit(w_in1 + n, *units[n])
                sp.wait_ge(g_lo, base(f"down{layer}", "g") + FT)
                gain_loads(nf)
                x_moves(nf, range(2))
                if layer == 0:
                    k_unit(w_in1 + 2, *units[2])
                x_moves(nf, range(2, NORM_TILES[nf] + 2))
                if layer == 0:
                    for n in range(3, len(units) - 2):
                        k_unit(w_in1 + n, *units[n])

        @block.tensor
        def _(pe):
            mm = nc.tensor.matmul

            def three(out_, s_hi, s_lo, m_hi, m_lo, start=True, stop=True):
                mm(out_, s_hi, m_hi, start=start, stop=False)
                mm(out_, s_hi, m_lo, start=False, stop=False)
                return mm(out_, s_lo, m_hi, start=False, stop=stop)

            def ring_free(r):
                at_least(pe, t_free, r - 1)

            def ada_mm(use, r, slot, inc=None):
                ring_free(r)
                pe.wait_ge(ada_in[slot], use * 32)
                o = bank(6 + slot, ADA_COLS)[0:2, :]
                for k in range(KC):
                    last = mm(o, silu[:, k, :], ada_raw[:, slot, k, :], start=k == 0, stop=k == KC - 1)
                last.then_inc(t_done, 1)

            def ada_across(r, slot, count):
                ring_free(r)
                pe.wait_ge(ada_summed, count)
                o = bank(6 + slot, ADA_COLS)[0:2, :]
                for v in range(2):
                    last = mm(o, stream[:, v, :], ada_sum[:, v, :], start=v == 0, stop=v == 1)
                last.then_inc(t_done, 1)

            def turn(r, rb, srcs, pn=P):
                if pn < P and not (isinstance(r, int) and r <= 1):
                    wait_apart(pe, (t_free, r - 1))
                else:
                    ring_free(r)
                for n, src in enumerate(srcs):
                    last = nc.tensor.transpose(bank(6 + rb % 2)[0:pn, n * P:(n + 1) * P], src, ident[:, :])
                last.then_inc(t_done, 1)

            def weights(u):
                pe.wait_ge(w_lo_done, u + 1)

            def norm_turns(name, first_unit=None):
                T = NORM_TILES[name]
                for t in range(T + (first_unit is not None)):
                    if t and first_unit is not None:
                        if t == T:
                            pe.wait_ge(t_free, base(name, "t") + 2 * t)
                            first_unit(t - 1)
                            break
                    pe.wait_ge(h_ready, base(name, "h") + t + 1)
                    for half in range(2):
                        r = base(name, "t") + 2 * t + half
                        turn(r, r, [h_tok[t % 2][:, (4 * half + k) * P:(4 * half + k + 1) * P] for k in range(4)])
                    if t and first_unit is not None:
                        pe.wait_ge(t_free, base(name, "t") + 2 * t)
                        first_unit(t - 1)

            last_use = [0] * 6

            def bank_free(b):
                at_least(pe, acc_evac, last_use[b])

            def unit_mm(slot, tiles, kn, n, lhs, k0, start, stop, wk0=0, after=None):
                wh = w_hi[:, slot, :]
                wl = w_lo[:, slot, :]
                for b, t in enumerate(tiles):
                    if len(tiles) == 1:
                        b = t
                    if start:
                        bank_free(b)
                    for k in range(kn):
                        rows = slice(t * P, (t + 1) * P)
                        cols = slice((wk0 + k) * n, (wk0 + k + 1) * n)
                        last = three(bank(b, n), lhs[0][:, k0 + k, rows], lhs[1][:, k0 + k, rows],
                                     wh[:, cols], wl[:, cols], start and k == 0, stop and k == kn - 1)
                    last.then_inc(mm_done, 1)
                    if after is not None:
                        after(b)

            def first_tile(layer, b):
                name = f"in{layer}"
                u = base(name, "w")
                _, cn, tiles = IN_CHUNKS[layer][0]
                if b == 0:
                    weights(u)
                if b in tiles:
                    unit_mm(u % 2, [b], 4, cn, (act_hi, act_lo), 0, True, False)

            def in_projection(layer):
                name = f"in{layer}"
                u, ev = base(name, "w"), base(name, "ev")
                pe.wait_ge(t_free, base(name, "t"))
                t0 = base(name, "t")
                for ci, (c0, cn, tiles) in enumerate(IN_CHUNKS[layer]):
                    for n in range(2):
                        if ci == n == 0:
                            u += 1
                            continue
                        weights(u)
                        after = None
                        if layer == 0 and ci == 2 and n == 0:
                            def after(b):
                                pe.wait_ge(staged, b + 1)
                                turn(t0 + 8 + b, t0 + 8 + b,
                                     [mla_in[b][:, k * P:(k + 1) * P] for k in range(3)])
                        unit_mm(u % 2, tiles, 4, cn, (act_hi, act_lo), 4 * n, n == 0, n == 1, after=after)
                        if layer == 0:
                            for v in range(0 if u == 1 else u, u + 1):
                                for k in range(2):
                                    g = ADA_FIRST + 2 * v + k
                                    ada_mm(g // 2 + 1, ada_round(0, g), k)
                        u += 1
                    for b in range(len(tiles)):
                        last_use[b] = ev + b + 1
                    ev += len(tiles)
                if layer == 0:
                    pe.wait_ge(t_free, t0 + 14)
                    for kn, k0, n in ((2, 0, 384), (1, 2, 512)):
                        weights(u)
                        for half in range(2):
                            wh = w_hi[:, u % 2, 0:kn * 2 * n].rearrange("p (k c) -> p k c", k=kn)
                            wl = w_lo[:, u % 2, 0:kn * 2 * n].rearrange("p (k c) -> p k c", k=kn)
                            for b in range(NT):
                                bank_free(b)
                                last_use[b] = ev + b + 1
                                for k in range(kn):
                                    rows = slice(b * P, (b + 1) * P)
                                    cols = slice(half * n, (half + 1) * n)
                                    last = three(bank(b, n), lat_t[0][:, k0 + k, rows], lat_t[1][:, k0 + k, rows],
                                                 wh[:, k, cols], wl[:, k, cols], k == 0, k == kn - 1)
                                last.then_inc(mm_done, 1)
                            ev += NT
                        for k in range(2):
                            g = ADA_FIRST + 2 * u + k
                            ada_mm(g // 2 + 1, ada_round(0, g), k)
                        u += 1

            def attention(name, a):
                T0, S0, H0 = base(name, "t"), base(name, "s"), base(name, "hd")
                d, dv = a.d, a.dv

                def prep(h, s, rounds):
                    for n in rounds:
                        raw = (q_raw, k_raw)[n // 2][s][:, 0:NT * d].rearrange("p (t c) -> p t c", c=d)
                        tiles = (a.q_rounds, a.k_rounds)[n // 2][n % 2]
                        r = a.prep_round(h, n) + T0
                        turn(r, a.prep_round(0 if isinstance(h, int) and h == 0 else 2 + s, n) + T0,
                             [raw[:, t, :] for t in tiles], d)

                def scores(h, s, j):
                    t, lo, n, _ = a.units[j]
                    rows = slice(t * P, (t + 1) * P)
                    sb0 = (j % 2) * 2
                    regions = []
                    if n:
                        regions.append((bank(sb0, n * P), slice(lo * P, (lo + n) * P)))
                    regions.append((bank(sb0 + 1, CTX), slice(LAT, ROWS)))
                    q, k = qt[s], kt[s]
                    for qi, ki, start, stop in ((0, 0, True, False), (0, 1, False, False), (1, 0, False, True)):
                        for o, keys in regions:
                            last = mm(o, q[qi][0:d, rows], k[ki][0:d, keys], start=start, stop=stop)
                    last.then_inc(s_done, 1)

                def probs_t(h, j, last_head):
                    r = a.unit_round(h, j, last_head) + T0
                    for n, chunks in enumerate(a.units[j][3]):
                        turn(r + n, a.unit_round(0, j, last_head) + T0 + n,
                             [prob[j % 2][:, c:c + P] for c, _ in chunks])

                def pv(h, s, j):
                    chunks = [c for rnd in a.units[j][3] for c in rnd]
                    t = a.units[j][0]
                    b = 4 if a.full else 4 + s
                    o = ps[0:dv, b * 512 + t * P:b * 512 + (t + 1) * P]
                    for n, (_, key) in enumerate(chunks):
                        last = three(o, vs[s][0][:, key, 0:dv], vs[s][1][:, key, 0:dv],
                                     pt[j % 2][0][:, n, :], pt[j % 2][1][:, n, :], n == 0, n == len(chunks) - 1)
                    last.then_inc(pv_done, 1)

                def step(i, s, j, last_pair, first=False):
                    h = i * 2 + s
                    last_head = last_pair and s == 1
                    unit = h * a.nu + (S0 + j)
                    j2, s2, h2 = j + 2, s, h
                    if j2 >= a.nu:
                        j2, s2, h2 = j2 - a.nu, 1 - s, h + 1
                    if not (last_head and s2 != s):
                        if j2 == 0:
                            pe.wait_ge(t_free, a.prep_end(h2) + T0)
                        pe.wait_ge(exp_done, unit + 1)
                        scores(h2, s2, j2)
                    pe.wait_ge(p_scaled, unit + 1)
                    probs_t(h, j, last_head)
                    if not first:
                        pj, p_s, ph = (j - 1, s, h) if j else (a.nu - 1, 1 - s, h - 1)
                        pv_of(ph, p_s, pj, last_head and j > 0)
                    if a.prep_rounds[j] and not last_head:
                        if 0 in a.prep_rounds[j]:
                            wait_head(i, s)
                        prep(h + 1, 1 - s, a.prep_rounds[j])

                def wait_head(i, s):
                    fills = head_fills[name]
                    if s == 0:
                        pe.wait_ge(head_in[1], i * a.load_inc + (fills[1] + a.load_inc))
                    else:
                        pe.wait_ge(head_in[0], i * a.load_inc + (fills[0] + 2 * a.load_inc))

                def pv_of(h, s, j, last_head):
                    pe.wait_ge(t_free, a.unit_round(h, j, last_head) + (T0 + a.unit_rounds[j]))
                    if j == 0:
                        pe.wait_ge(v_split, h + (H0 + 1))
                        pe.wait_ge(o_lo, h + (H0 + OL0 - (0 if a.full else 1)))
                    pv(h, s, j)

                at_least(pe, acc_evac, base(name, "ev"))
                at_least(pe, o_lo, OL0 + H0)
                pe.wait_ge(head_in[0], head_fills[name][0] + a.load_inc)
                prep(0, 0, range(4))
                pe.wait_ge(t_free, T0 + 4)
                for j in range(2):
                    at_least(pe, exp_done, S0)
                    scores(0, 0, j)
                step(0, 0, 0, False, first=True)

                def body(i):
                    for s in range(2):
                        for j in range(a.nu):
                            if s or j:
                                step(i, s, j, False)
                    step(i + 1, 0, 0, False)
                run_loop(pe, 0, a.pairs - 1, body)
                i = a.pairs - 1
                for s in range(2):
                    for j in range(a.nu):
                        if s or j:
                            step(i, s, j, True)
                pv_of(a.heads - 1, 1, a.nu - 1, True)

            def out_projection(layer):
                name = f"out{layer}"
                u, ev = base(name, "w"), base(name, "ev")
                tiles = range(ROWT[layer])
                pe.wait_ge(o_lo, OL0 + base(name, "hd"))
                for half in range(2):
                    for n in range(2):
                        weights(u)
                        unit_mm(u % 2, tiles, 4, 512, (act_hi, act_lo), 4 * n, n == 0, n == 1)
                        u += 1
                    for b in tiles:
                        last_use[b] = ev + b + 1
                    ev += len(tiles)

            def feed_up(layer):
                name = f"up{layer}"
                F0, U0, full = base(name, "f"), base(name, "w"), layer == 0
                pe.wait_ge(t_free, base(name, "t"))
                pe.wait_ge(acc_evac, base(name, "ev"))

                def product(half, slot):
                    b = 3 * slot
                    wh = w_hi[:, slot, half * 1024:(half + 1) * 1024].rearrange("p (k c) -> p k c", k=KC)
                    wl = w_lo[:, slot, half * 1024:(half + 1) * 1024].rearrange("p (k c) -> p k c", k=KC)
                    regions = [(bank(b + 2 * half), slice(0, LAT))]
                    if full:
                        regions.append((bank(b + 1, CTX, CTX * half), slice(LAT, ROWS)))
                    for k in range(KC):
                        for wt, m, st, sp_ in ((wh, act_hi, k == 0, False), (wh, act_lo, False, False),
                                               (wl, act_hi, False, k == KC - 1)):
                            for o, rows in regions:
                                last = mm(o, wt[:, k, :], m[:, k, rows], start=st, stop=sp_)
                    last.then_inc(mm_done, 1)

                def tile(i, k, free):
                    pe.wait_ge(w_lo_done, i * 2 + (U0 + k + 1))
                    if free:
                        pe.wait_ge(gated, i * 2 + (F0 + k - 1))
                    product(0, k)
                    product(1, k)
                    if full:
                        ada_across(i * 2 + (base(name, "t") + k), k, i * 2 + (k + 1))

                for k in range(2):
                    tile(0, k, False)
                run_loop(pe, 1, FT // 2, lambda i: [tile(i, k, True) for k in range(2)])

            def feed_down(layer):
                name = f"down{layer}"
                U0, G0, ev = base(name, "w"), base(name, "g"), base(name, "ev")
                tiles = range(ROWT[layer])
                pe.wait_ge(gated, base(name, "f"))
                H = FT // 2
                for half in range(2):
                    def unit(i, k, start=False, stop=False):
                        n = half * H + 1 + k
                        pe.wait_ge(w_lo_done, i * 2 + (U0 + n + 1))
                        pe.wait_ge(g_lo, i * 2 + (G0 + n + 1))
                        s = n % 2
                        unit_mm(s, tiles, 2, 512, (act_hi, act_lo), 2 * s, start, stop)
                    unit(0, -1, start=True)
                    run_loop(pe, 0, 2, lambda i: [unit(i, k) for k in range(2)])
                    if layer == half == 0:
                        ada_across(ada_round(1, FT), 0, FT + 1)
                    run_loop(pe, 2, (H - 3) // 2, lambda i: [unit(i, k) for k in range(2)])
                    unit((H - 3) // 2, 0)
                    if layer == half == 0:
                        ada_across(ada_round(1, FT + 1), 1, FT + 2)
                    unit((H - 3) // 2, 1, stop=True)
                    for b in tiles:
                        last_use[b] = ev + b + 1
                    ev += len(tiles)

            pe.wait_ge(sc_ready, 1)
            mm(bank(0, 2)[0:2, :], silu[:, 0, :], silu[:, 0, :], start=True, stop=True).then_inc(pv_done, 1)
            for g in range(ADA_FIRST):
                ada_mm(g // 2 + 1, g, g % 2)
            pe.wait_ge(const_in, CONST_IN)
            norm_turns("norm0", lambda t: first_tile(0, t))
            in_projection(0)
            attention("mla", MLA)
            attention("swa", SWA)
            out_projection(0)
            norm_turns("norm1")
            feed_up(0)
            feed_down(0)
            norm_turns("norm2", lambda t: first_tile(1, t))
            in_projection(1)
            attention("na", NA)
            attention("gqa", GQA)
            out_projection(1)
            norm_turns("norm3")
            feed_up(1)
            feed_down(1)

        @block.scalar
        def _(act):
            A = nc.scalar.activation
            own = Chain(act, act_self)

            for dst, src in CVEC:
                act.dma_start(dst, src, allow_slow_non_contiguous=True).then_inc(c_in, 16)
            act.wait_ge(c_in, 16)
            A(cexp[:, :, :], cvec[:, :, :], ACT.Exp, scale=-1.0).then_inc(act_self, 1)
            own.n += 1
            for dst, src in CONSTS:
                act.dma_start(dst, src, allow_slow_non_contiguous=True).then_inc(const_in, 16)
            act.wait_ge(const_in, CONST_IN)

            def split_hi(u, s, n, per=None):
                A(w_hi[:, s, 0:n], w_raw[:, s, 0:n], ACT.Copy).then_inc(w_hi_done, 1)

            def w_loaded(u):
                act.wait_ge(w_in[u % 2], 32 * (u // 2 + 1))

            def norm(name, late=None):
                y, h = NORMS[name][0] is not None, NORMS[name][1] is not None
                T = NORM_TILES[name]
                squared = []

                def square(src, sum_, sem_, count):
                    n = len(squared)
                    if n >= 2:
                        act.wait_ge(*squared[n - 2])
                    squared.append((sem_, count))
                    A(kilo(12 + n % 2), src, ACT.Square, accum_out=sum_).then_inc(sem_, 1)
                if y and "g" in BASE[name]:
                    act.wait_ge(g_lo, base(name, "g"))
                for t in range(T + 2):
                    if y and t < T:
                        act.wait_ge(mm_done, base(name, "mm") - T + t + 1)
                        A(Y[:, t, 512:1024], bank(t), ACT.Copy).then_inc(acc_evac, 1)
                        act.wait_ge(acc_evac, base(name, "ev") - T + t + 1)
                        square(Y[:, t, :], ssy[:, t:t + 1], sum_y, base(name, "y") + t + 1)
                    if t == T and late is not None:
                        late()
                    if h and 1 <= t <= T:
                        q = t - 1
                        if y:
                            act.wait_ge(x_added, base(name, "y") + q + 1)
                            src = x_new[q % 2]
                        else:
                            act.wait_ge(x_ld[q % 2], 16 * (base(name, "xl") // 2 + q // 2 + 1))
                            src = x_in[q % 2]
                        square(src, ssx[:, q:q + 1], sum_x, base(name, "h") + q + 1)
                    if h and t >= 2:
                        q = t - 2
                        for half in range(2):
                            r = base(name, "t") + 2 * q + half
                            act.wait_ge(t_done, r + 1)
                            A(act_hi[:, 4 * half:4 * half + 4, q * P:(q + 1) * P],
                              bank(6 + r % 2).rearrange("p (k r) -> p k r", k=4), ACT.Copy).then_inc(t_hi, 1)

            def projection_splits(units, u0, mm0, tiles_of, between=None):
                done = mm0
                for n, size in enumerate(units):
                    if between is not None:
                        between(n)
                    done += tiles_of[n]
                    act.wait_ge(mm_done, done)
                    w_loaded(u0 + n + 2)
                    split_hi(u0 + n + 2, (u0 + n) % 2, size)

            def latents(n):
                if n != 4:
                    return
                for b in range(NT):
                    r = base("in0", "t") + 8 + b
                    act.wait_ge(t_done, r + 1)
                    A(lat_t[0][:, :, b * P:(b + 1) * P],
                      bank(6 + r % 2, 3 * P).rearrange("p (k r) -> p k r", k=3), ACT.Copy).then_inc(t_hi, 1)

            def attention(name, a):
                T0, S0, H0 = base(name, "t"), base(name, "s"), base(name, "hd")
                d, dv = a.d, a.dv

                def prep(h, hs, s, rounds):
                    for n in rounds:
                        dst = (qt, kt)[n // 2][s][0]
                        tiles = (a.q_rounds, a.k_rounds)[n // 2][n % 2]
                        act.wait_ge(t_done, a.prep_round(h, n) + (T0 + 1))
                        b = 6 + (T0 + a.prep_round(hs, n)) % 2
                        A(dst[0:d, tiles[0] * P:(tiles[-1] + 1) * P], bank(b, len(tiles) * P)[0:d, :], ACT.Copy)\
                            .then_inc(t_hi, 1)

                def probs_hi(h, j, last_head):
                    at = 0
                    for n, chunks in enumerate(a.units[j][3]):
                        act.wait_ge(t_done, a.unit_round(h, j, last_head) + (T0 + n + 1))
                        b = 6 + (T0 + a.unit_round(0, j, last_head) + n) % 2
                        A(pt[j % 2][0][:, at:at + len(chunks), :],
                          bank(b, len(chunks) * P).rearrange("p (k r) -> p k r", r=P), ACT.Copy).then_inc(t_hi, 1)
                        at += len(chunks)

                def exps(h, j, unit):
                    t, lo, n, _ = a.units[j]
                    p, sb0 = j % 2, (j % 2) * 2
                    wait_apart(act, (mx_done, unit + 1))
                    bias = nb[:, p:p + 1]
                    if a.sink:
                        A(es[:, p:p + 1], sinks[:, ds(h, 1)], ACT.Exp, bias=bias)
                    if a.bias and n:
                        A(prob[p][:, 0:n * P], biased[p][:, 0:n * P], ACT.Exp, bias=bias, scale=a.scale,
                          accum_out=ex[:, p, 0:1])
                        A(prob[p][:, LAT:ROWS], bank(sb0 + 1, CTX), ACT.Exp, bias=bias, scale=a.scale,
                          accum_out=ex[:, p, 1:2]).then_inc(exp_done, 1)
                    else:
                        c = 0 if n else LAT
                        A(prob[p][:, c:ROWS], ps[:, sb0 * 512 + c:sb0 * 512 + ROWS], ACT.Exp, bias=bias,
                          scale=a.scale, accum_out=ex[:, p, 0:1]).then_inc(exp_done, 1)

                def outputs(h, i, s):
                    b = 4 if a.full else 4 + s
                    off = (s * dv) % P
                    wait_apart(act, (pv_done, (h + 1) * a.nu + (S0 + PV0)))
                    k = i + a.mix_chunk if dv == 64 else h + a.mix_chunk
                    A(act_hi[off:off + dv, ds(k, 1), 0:a.acols].rearrange("p o r -> p (o r)"),
                      ps[0:dv, b * 512:b * 512 + a.acols], ACT.Copy).then_inc(o_hi, 1)

                def step(i, s, j, last_pair):
                    h = i * 2 + s
                    last_head = last_pair and s == 1
                    unit = h * a.nu + (S0 + j)
                    at_least(act, pv_done, unit + (PV0 - 1))
                    probs_hi(h, j, last_head)
                    j2, h2 = (j + 2, h) if j + 2 < a.nu else (j + 2 - a.nu, h + 1)
                    if not (last_head and j + 2 >= a.nu):
                        exps(h2, j2, unit + 2)
                    if j == 0 and not (isinstance(h, int) and h == 0):
                        outputs(h - 1, i - 1 if s == 0 else i, 1 - s)
                    if a.prep_rounds[j] and not last_head:
                        prep(h + 1, 2 + (1 - s), 1 - s, a.prep_rounds[j])

                prep(0, 0, 0, range(4))
                for j in range(2):
                    exps(0, j, S0 + j)
                if name == "na":
                    stages_stored(act, base(name, "st"))
                step(0, 0, 0, False)

                def body(i):
                    for s in range(2):
                        for j in range(a.nu):
                            if s or j:
                                step(i, s, j, False)
                    step(i + 1, 0, 0, False)
                run_loop(act, 0, a.pairs - 1, body)
                i = a.pairs - 1
                for s in range(2):
                    for j in range(a.nu):
                        if s or j:
                            step(i, s, j, True)
                outputs(a.heads - 1, i, 1)

            def out_projection(layer):
                name = f"out{layer}"
                T, mm0, u0 = ROWT[layer], base(name, "mm"), base(name, "w")
                for n in range(3):
                    if n == 1:
                        for t in range(T):
                            act.wait_ge(mm_done, mm0 + T + t + 1)
                            A(Y[:, t, 0:512], bank(t), ACT.Copy).then_inc(acc_evac, 1)
                    late_split(name, n, T, 2048)

            def late_split(name, n, T, size):
                act.wait_ge(mm_done, base(name, "mm") + (n + 1) * T)
                w_loaded(base(name, "w") + n + 2)
                split_hi(None, n % 2, size)

            def feed_up(layer):
                name = f"up{layer}"
                M0, U0, F0 = base(name, "mm"), base(name, "w"), base(name, "f")
                cols = ROWS if layer == 0 else LAT
                act.wait_ge(x_added, base(name, "y"))

                def tile(i, k, size, free):
                    wait_apart(act, (mm_done, i * 4 + (M0 + 2 * k + (2 if layer == 0 else 1))),
                               *([(gated, i * 2 + (F0 + k - 1))] if free else []))
                    c = conv_acc[:, k, 0:cols]
                    prm = conv[:, layer, ds(i * 2 + k, 1), :]
                    A(c, ps[:, 3 * k * 512:3 * k * 512 + cols], ACT.Identity,
                      scale=prm[:, 0, 1:2], bias=prm[:, 0, 3:4]).then_inc(centre, 1)
                    act.wait_ge(taps, i * 2 + (F0 + k + 1))
                    A(c, c, ACT.Gelu_apprx_tanh).then_inc(gelu, 1)
                    act.wait_ge(mm_done, i * 4 + (M0 + 2 * k + 2))
                    act.wait_ge(w_in[k], i * 32 + (32 * (U0 // 2) + 64))
                    split_hi(None, k, size)

                for k in range(2):
                    tile(0, k, 2048, False)
                run_loop(act, 1, FT // 2 - 1, lambda i: [tile(i, k, 2048, True) for k in range(2)])
                for k in range(2):
                    tile(FT // 2 - 1, k, 1024, True)

            def feed_down(layer, after):
                name = f"down{layer}"
                T, cols = ROWT[layer], (ROWS if layer == 0 else LAT)
                M0, U0, G0, W0 = base(name, "mm"), base(name, "w"), base(name, "g"), base(name, "w")
                H = FT // 2

                def g_split(chunk, s):
                    A(act_hi[:, 2 * s:2 * s + 2, 0:cols], G[:, ds(chunk, 2), 0:cols], ACT.Copy).then_inc(g_hi, 1)

                act.wait_ge(mm_done, M0)
                act.wait_ge(gated, base(name, "f"))
                for n in range(2):
                    g_split(2 * n, n)

                def step(i, k, half, c, w=1024, g=True):
                    n = c + k
                    done = (mm_done, i * (2 * T) + (M0 + (n + 1) * T))
                    if w:
                        wait_apart(act, done, (w_in[n % 2], i * 32 + 32 * ((U0 + n + 2) // 2 + 1)))
                        split_hi(None, n % 2, w)
                    else:
                        wait_apart(act, done)
                    if g:
                        m = n + 2 - (H if n + 2 >= H and half is None else 0)
                        g_split(i * 4 + 2 * ((n + 2) % H if half is None else n + 2 - half * H), n % 2)

                run_loop(act, 0, 4, lambda i: [step(i, k, 0, 0) for k in range(2)])
                step(0, 0, 0, 8)
                step(0, 0, None, 9)
                for t in range(T):
                    act.wait_ge(mm_done, M0 + 10 * T + t + 1)
                    A(Y[:, t, 0:512], bank(t), ACT.Copy).then_inc(acc_evac, 1)
                step(0, 0, None, 10)
                run_loop(act, 0, 4, lambda i: [step(i, k, 1, 11) for k in range(2)])
                step(0, 0, 1, 19)
                if after:
                    late_split(name, FT - 2, T, after)

            for u in range(2):
                w_loaded(u)
                split_hi(u, u, 4 * MLA_IN)
            norm("norm0")
            sizes = [4 * 512] * 2 + [4 * 256] * 2 + [2 * 8 * MLA_D, 16 * NOPE] + [2048] * 2
            projection_splits(sizes, 0, 0, [NT] * 6 + [2 * NT] * 2, latents)
            attention("mla", MLA)
            attention("swa", SWA)
            out_projection(0)
            norm("norm1", lambda: late_split("out0", 3, NT, 2048))
            feed_up(0)
            feed_down(0, 2048)
            norm("norm2", lambda: late_split("down0", FT - 1, NT, 2048))
            tiles = [len(c[2]) for c in IN_CHUNKS[1] for _ in range(2)]
            projection_splits([2048] * 10, base("in1", "w"), base("in1", "mm"), tiles)
            attention("na", NA)
            attention("gqa", GQA)
            out_projection(1)
            norm("norm3", lambda: late_split("out1", 3, LT, 2048))
            feed_up(1)
            feed_down(1, None)
            norm("norm4")

        @block.vector
        def _(dve):
            V = nc.vector
            own = Chain(dve, dve_self)

            def minus_hi(out_, full, hi, sem_):
                V.tensor_sub(out_, full, hi.bitcast(fp32)).then_inc(sem_, 1)

            def split_lo(u, s, n):
                dve.wait_ge(w_hi_done, u + 1)
                minus_hi(w_lo[:, s, 0:n], w_raw[:, s, 0:n], w_hi[:, s, 0:n], w_lo_done)

            def ada_evac(r, slot, use):
                dve.wait_ge(t_done, r + 1)
                at_least(dve, ada_out[slot], (use - 1) * 16)
                V.tensor_add(ada_row[:, slot, :], bank(6 + slot, ADA_COLS)[0:2, :], ada_bias[:, slot, :])\
                    .then_inc(t_free, 1)

            def modulation(name):
                gate, scale = NORMS[name][:2]
                y, h = gate is not None, scale is not None
                streams = range(NORM_STREAMS[name])
                dve.wait_ge(mod_in, 16 * (base(name, "mod") + len(streams) * (y + 2 * h)))
                dve.wait_ge(gain_in, 16 * (base(name, "gain") + y + h))
                for v in streams:
                    if y:
                        own.inc(V.tensor_mul(mod_row[0][v], mod_row[0][v], h_tok[0]))
                    if h:
                        own.inc(V.scalar_tensor_tensor(out=mod_row[1][v], in0=mod_row[1][v], scalar=1.0,
                                                       in1=h_tok[1], op0=ALU.add, op1=ALU.mult))

            def ada_multiply(slot, use):
                dve.wait_ge(ada_in[slot], use * 32)
                for k in range(KC):
                    for v in range(2):
                        w, x = ada_raw[:, slot, k, :], silu[:, k, v:v + 1]
                        if k:
                            last = k == KC - 1 and v == 1
                            dve.wait_ge(dve_self, own.term + (own.n - (0 if last else 1)))
                            ins = V.scalar_tensor_tensor(out=ada_sum[:, v, :], in0=w, scalar=x,
                                                         in1=ada_sum[:, v, :], op0=ALU.mult, op1=ALU.add)
                        else:
                            ins = V.tensor_scalar(ada_sum[:, v, :], w, x, None, ALU.mult)
                        if k == KC - 1 and v == 1:
                            ins.then_inc(ada_summed, 1)
                        else:
                            own.inc(ins)

            def norm(name, late=None):
                y, h = NORMS[name][0] is not None, NORMS[name][1] is not None
                T, T0, H0, Y0 = NORM_TILES[name], base(name, "t"), base(name, "h"), base(name, "y")
                own.wait()
                for t in range(T + 2):
                    if y and t < T:
                        dve.wait_ge(rs_y, Y0 + t + 1)
                        V.scalar_tensor_tensor(out=Y[:, t, :], in0=Y[:, t, :], scalar=rsy[:, t:t + 1],
                                               in1=mod_row[0][t // LT], op0=ALU.mult, op1=ALU.mult)\
                            .then_inc(y_scaled, 1)
                    if t == T and late is not None:
                        late()
                    if h and 1 <= t <= T:
                        q = t - 1
                        dve.wait_ge(rs_x, H0 + q + 1)
                        if q >= 2:
                            dve.wait_ge(t_done, T0 + 2 * (q - 2) + 2)
                        src = x_new[q % 2] if y else x_in[q % 2]
                        V.scalar_tensor_tensor(out=h_tok[q % 2], in0=src, scalar=rsx[:, q:q + 1],
                                               in1=mod_row[1][q // LT], op0=ALU.mult, op1=ALU.mult)\
                            .then_inc(h_scaled, 1)
                    if h and t >= 2:
                        q = t - 2
                        for half in range(2):
                            r = T0 + 2 * q + half
                            dve.wait_ge(t_hi, base(name, "th") + 2 * q + half + 1)
                            cols = (slice(None), slice(4 * half, 4 * half + 4), slice(q * P, (q + 1) * P))
                            minus_hi(act_lo[cols], bank(6 + r % 2).rearrange("p (k r) -> p k r", k=4),
                                     act_hi[cols], t_free)
                    if h and 1 <= t <= T:
                        q = t - 1
                        dve.wait_ge(h_scaled, H0 + q + 1)
                        V.tensor_add(h_tok[q % 2], h_tok[q % 2], mod_row[2][q // LT]).then_inc(h_ready, 1)

            def apply_rope(view, tile, w, sem_):
                nh = view.shape[1]
                x = view.rearrange("p h (s w) -> p h s w", s=2)
                a, b = (t[:, 0:nh * 2 * w].rearrange("p (h s w) -> p h s w", h=nh, s=2) for t in tmp)
                cos, sin = (rope[w][:, tile, n, :].unsqueeze(1).unsqueeze(1).to_broadcast([P, nh, 2, w])
                            for n in range(2))
                own.inc(V.tensor_mul(a, x, cos))
                own.inc(V.tensor_mul(b, x, sin))
                own.wait()
                own.inc(V.tensor_sub(x[:, :, 0, :], a[:, :, 0, :], b[:, :, 1, :]))
                last = V.tensor_add(x[:, :, 1, :], a[:, :, 1, :], b[:, :, 0, :])
                if sem_ is None:
                    own.inc(last)
                else:
                    own.wait()
                    last.then_inc(sem_, 1)

            mm_seen, staged_q, ev_norm = [0], [0], [0]

            def chunk(name, tiles, n, norms, gains, ropes, latent=False):
                tiles = list(tiles)
                slots = []

                def evac(x, t):
                    dve.wait_ge(mm_done, mm_seen[0] + x + 1)
                    if latent:
                        dst = mla_in[t]
                    else:
                        s = staged_q[0] % 4
                        at_least(dve, stage_out[s], 16 * (staged_q[0] // 4))
                        dst = stage[s][:, 0:n]
                        staged_q[0] += 1
                    slots.append(dst)
                    last = V.tensor_copy(dst, bank(x, n))
                    last.then_inc(acc_evac, 1)
                    evacs[0] += 1
                    if norms:
                        p = ev_norm[0] % 2
                        if ev_norm[0] >= 2:
                            dve.wait_ge(head_rs, ev_norm[0] - 1)
                        ev_norm[0] += 1
                        dve.wait_ge(acc_evac, evacs[0])
                        for k, (c, w) in enumerate(norms):
                            ins = V.tensor_tensor_reduce(out=tmp[k % 2][:, 0:w], in0=dst[:, c:c + w],
                                                         in1=dst[:, c:c + w], scale=1.0, scalar=0.0,
                                                         op0=ALU.mult, op1=ALU.add,
                                                         accum_out=ssh[:, p, k:k + 1])
                            if k < len(norms) - 1:
                                own.inc(ins)
                                own.wait()
                        ins.then_inc(squares, 1)

                def finish(x, t):
                    dst = slots[x]
                    rp = [r for r in ropes if t < LT]
                    if norms:
                        k0 = ev_norm[0] - (len(slots) - x)
                        dve.wait_ge(head_rs, k0 + 1)
                        p = k0 % 2
                        for k, (c, w) in enumerate(norms):
                            ins = V.scalar_tensor_tensor(out=dst[:, c:c + w], in0=dst[:, c:c + w],
                                                         scalar=rsh[:, p, k:k + 1], in1=gains[k],
                                                         op0=ALU.mult, op1=ALU.mult)
                            own.inc(ins)
                        own.wait()
                    else:
                        dve.wait_ge(acc_evac, evacs[0] - (len(slots) - 1 - x))
                    for k, (view, w) in enumerate(rp):
                        apply_rope(view(dst), t, w, None)
                    if norms or rp:
                        own.wait()

                for x, t in enumerate(tiles):
                    evac(x, t)
                    if norms and x:
                        finish(x - 1, tiles[x - 1])
                        mark()
                    if not norms:
                        finish(x, t)
                        mark()
                if norms:
                    finish(len(tiles) - 1, tiles[-1])
                    mark()
                mm_seen[0] += len(tiles)

            evacs = [0]

            def mark():
                V.tensor_copy(flag[:, 0:1], mhalf[:, 0:1]).then_inc(staged, 1)

            def in_projection(layer):
                name = f"in{layer}"
                W0 = base(name, "w")
                evacs[0] = base(name, "ev")
                mm_seen[0] = base(name, "mm")
                staged_q[0] = base(name, "st")

                def heads_of(c, nh, d, a=0, b=None):
                    return lambda v: v[:, c:c + nh * d].rearrange("p (h d) -> p h d", d=d)[:, :, a:b]
                if layer == 0:
                    todo = [
                        dict(n=MLA_IN, norms=[(0, Q_RANK), (Q_RANK, KV_RANK)],
                             gains=[g_mla[:, 0:Q_RANK], g_mla[:, Q_RANK:]],
                             ropes=[(heads_of(Q_RANK + KV_RANK, 1, ROPE_D), 16)], latent=True),
                        dict(n=512, norms=[], gains=[], ropes=[(heads_of(0, 8, 64), 32)]),
                        dict(n=256, norms=[], gains=[], ropes=[(heads_of(0, 2, 64), 32)]),
                    ]
                    sizes = [2048] * 2 + [1024] * 2 + [2 * 8 * MLA_D, 16 * NOPE] + [2048] * 2
                else:
                    todo = [dict(n=512, norms=[], gains=[], ropes=[])] * 3 + [
                        dict(n=512, norms=[(k * P, P) for k in range(4)], gains=[g_gqa[:, 0, :]] * 4,
                             ropes=[(heads_of(0, 4, P), 64)]),
                        dict(n=512, norms=[(k * P, P) for k in range(2)], gains=[g_gqa[:, 1, :]] * 2,
                             ropes=[(heads_of(0, 2, P), 64)]),
                    ]
                    sizes = [2048] * 10
                n = 0

                def splits_and_ada():
                    split_lo(W0 + n + 2, n % 2, sizes[n])
                    if layer == 0:
                        for k in range(2):
                            g = ADA_FIRST + 2 * n + k
                            ada_evac(ada_round(0, g), k, g // 2 + 1)
                for spec, (_, _, tiles) in zip(todo, IN_CHUNKS[layer]):
                    mm_seen[0] += len(tiles)
                    if layer == 0 and n == 4:
                        for b in range(NT):
                            dve.wait_ge(t_hi, base("in0", "th") + b + 1)
                            r = base("in0", "t") + 8 + b
                            rows = slice(b * P, (b + 1) * P)
                            minus_hi(lat_t[1][:, :, rows], bank(6 + r % 2, 3 * P).rearrange("p (k r) -> p k r", k=3),
                                     lat_t[0][:, :, rows], t_free)
                    splits_and_ada()
                    n += 1
                    chunk(name, tiles, **spec)
                    splits_and_ada()
                    n += 1
                if layer == 0:
                    for kn, cols, ropes in ((2, 384, [(heads_of(0, 4, MLA_D, NOPE, MLA_D), 16)]), (1, 512, [])):
                        for half in range(2):
                            chunk(name, range(NT), cols, [], [], ropes)
                        splits_and_ada()
                        n += 1

            def attention(name, a):
                T0, TH0, S0, H0 = (base(name, k) for k in ("t", "th", "s", "hd"))
                d, dv = a.d, a.dv
                dT = TH0 - T0

                def prep(h, hs, s, rounds):
                    for n in rounds:
                        hi, lo = (qt, kt)[n // 2][s]
                        tiles = (a.q_rounds, a.k_rounds)[n // 2][n % 2]
                        dve.wait_ge(t_hi, a.prep_round(h, n) + (TH0 + 1))
                        b = 6 + (T0 + a.prep_round(hs, n)) % 2
                        cols = slice(tiles[0] * P, (tiles[-1] + 1) * P)
                        minus_hi(lo[0:d, cols], bank(b, len(tiles) * P)[0:d, :], hi[0:d, cols], t_free)

                def probs_lo(h, j, last_head):
                    at = 0
                    for n, chunks in enumerate(a.units[j][3]):
                        dve.wait_ge(t_hi, a.unit_round(h, j, last_head) + (TH0 + n + 1))
                        b = 6 + (T0 + a.unit_round(0, j, last_head) + n) % 2
                        sl = (slice(None), slice(at, at + len(chunks)), slice(None))
                        minus_hi(pt[j % 2][1][sl], bank(b, len(chunks) * P).rearrange("p (k r) -> p k r", r=P),
                                 pt[j % 2][0][sl], t_free)
                        at += len(chunks)

                def maxima(h, s, j, unit):
                    t, lo, n, _ = a.units[j]
                    p, sb0 = j % 2, (j % 2) * 2
                    wait_apart(dve, (s_done, unit + 1),
                               *([(bias_ready, h + 1)] if a.bias == "na" and n else []))
                    m0, m1 = mx[:, p, 0:1], mx[:, p, 1:2]
                    if a.bias and n:
                        if a.bias == "na":
                            bias = na_bias[s][:, (6 - 2 * t) * GRID_W:(6 - 2 * t) * GRID_W + LAT]
                        else:
                            bias = band[:, (lo - t + 1) * P:(lo - t + 1 + n) * P]
                        V.tensor_tensor_reduce(out=biased[p][:, 0:n * P], in0=bank(sb0, n * P), in1=bias,
                                               scale=1.0, scalar=-3.4e38, op0=ALU.add, op1=ALU.max, accum_out=m0)
                        own.inc(V.reduce_max(m1, bank(sb0 + 1, CTX), AX.X))
                        own.wait()
                    else:
                        c = 0 if n else LAT
                        own.inc(V.reduce_max(m0, ps[:, sb0 * 512 + c:sb0 * 512 + ROWS], AX.X))
                        own.wait()
                    second = m1 if a.bias and n else m0
                    if a.sink:
                        own.inc(V.scalar_tensor_tensor(out=m0, in0=m0, scalar=second, in1=sinks8[:, ds(h, 1)],
                                                       op0=ALU.max, op1=ALU.max))
                        own.wait()
                        second = m0
                    V.tensor_scalar(nb[:, p:p + 1], m0, second, -a.scale, ALU.max, ALU.mult).then_inc(mx_done, 1)

                def sums(j, unit):
                    n, p = a.units[j][2], j % 2
                    dve.wait_ge(exp_done, unit + 1)
                    src = ex[:, p, 0:1]
                    if a.bias and n:
                        own.inc(V.tensor_add(rsum[:, p:p + 1], src, ex[:, p, 1:2]))
                        own.wait()
                        src = rsum[:, p:p + 1]
                    if a.sink:
                        own.inc(V.tensor_add(rsum[:, p:p + 1], src, es[:, p:p + 1]))
                        own.wait()
                        src = rsum[:, p:p + 1]
                    V.reciprocal(rinv[:, p:p + 1], src).then_inc(rc_done, 1)

                def outputs(h, i, s):
                    b = 4 if a.full else 4 + s
                    off = (s * dv) % P
                    dve.wait_ge(o_hi, h + (H0 + 1))
                    k = i + a.mix_chunk if dv == 64 else h + a.mix_chunk
                    sl = (slice(off, off + dv), ds(k, 1), slice(0, a.acols))
                    minus_hi(act_lo[sl].rearrange("p o r -> p (o r)"), ps[0:dv, b * 512:b * 512 + a.acols],
                             act_hi[sl].rearrange("p o r -> p (o r)"), o_lo)

                def step(i, s, j, last_pair):
                    h = i * 2 + s
                    last_head = last_pair and s == 1
                    unit = h * a.nu + (S0 + j)
                    j2, s2, h2 = (j + 2, s, h) if j + 2 < a.nu else (j + 2 - a.nu, 1 - s, h + 1)
                    ahead = not (last_head and j + 2 >= a.nu)
                    if ahead:
                        maxima(h2, s2, j2, unit + 2)
                    if not (last_head and j + 1 >= a.nu):
                        sums((j + 1) % a.nu, unit + 1)
                    probs_lo(h, j, last_head)
                    if j == 0 and not (isinstance(h, int) and h == 0):
                        outputs(h - 1, i - 1 if s == 0 else i, 1 - s)
                    if a.prep_rounds[j] and not last_head:
                        prep(h + 1, 2 + (1 - s), 1 - s, a.prep_rounds[j])

                prep(0, 0, 0, range(4))
                for j in range(2):
                    maxima(0, 0, j, S0 + j)
                    if j == 0:
                        sums(j, S0 + j)
                if name == "na":
                    stages_stored(dve, base(name, "st"))
                step(0, 0, 0, False)
                grow = 0
                for u in a.units:
                    biased_unit = bool(a.bias and u[2])
                    grow += 1 + (1 if a.sink else 0) + (1 if biased_unit else 0) + (1 if a.sink else 0)

                def body(i):
                    for s in range(2):
                        for j in range(a.nu):
                            if s or j:
                                step(i, s, j, False)
                    step(i + 1, 0, 0, False)
                run_loop(dve, 0, a.pairs - 1, body, own, 2 * grow)
                i = a.pairs - 1
                for s in range(2):
                    for j in range(a.nu):
                        if s or j:
                            step(i, s, j, True)
                outputs(a.heads - 1, i, 1)

            def out_projection(layer):
                for n in range(3):
                    split_lo(base(f"out{layer}", "w") + n + 2, n % 2, 2048)
                    if n == 0:
                        modulation(("norm1", "norm3")[layer])

            def feed_up(layer):
                name = f"up{layer}"
                M0, U0, F0, T0 = (base(name, k) for k in ("mm", "w", "f", "t"))
                full = layer == 0
                cols = ROWS if full else LAT
                for s in range(2):
                    dve.wait_ge(x_st[s], 16 * base(name, "xs") // 2)
                if full:
                    ada_multiply(0, ADA_UNITS // 2 + 1)

                def tile(i, k, size, ada=full):
                    prm = conv[:, layer, ds(i * 2 + k, 1), :]
                    c, g = conv_acc[:, k, :], ps[:, 3 * k * 512:3 * k * 512 + cols]
                    segments = [(0, LAT)] + ([(LAT, ROWS)] if full else [])
                    dve.wait_ge(centre, i * 2 + (F0 + k + 1))
                    for a, b in segments:
                        own.inc(V.scalar_tensor_tensor(out=c[:, a + 1:b], in0=g[:, a:b - 1], scalar=prm[:, 0, 0:1],
                                                       in1=c[:, a + 1:b], op0=ALU.mult, op1=ALU.add))
                    own.wait()
                    for a, b in segments:
                        last = V.scalar_tensor_tensor(out=c[:, a:b - 1], in0=g[:, a + 1:b], scalar=prm[:, 0, 2:3],
                                                      in1=c[:, a:b - 1], op0=ALU.mult, op1=ALU.add)
                    last.then_inc(taps, 1)
                    dve.wait_ge(gelu, i * 2 + (F0 + k + 1))
                    dve.wait_ge(mm_done, i * 4 + (M0 + 2 * k + 2))
                    dst = G[:, ds(i * 2 + k, 1), :].rearrange("p o r -> p (o r)")
                    if full:
                        V.tensor_mul(dst[:, LAT:ROWS], c[:, LAT:ROWS], bank(3 * k + 1, CTX, CTX))
                    V.tensor_mul(dst[:, 0:LAT], c[:, 0:LAT], bank(3 * k + 2)).then_inc(gated, 1)
                    split_lo(i * 2 + (U0 + k + 2), k, size)
                    if ada:
                        ada_evac(i * 2 + (T0 + k), k, i + (ADA_UNITS // 2 + 1))
                        ada_multiply(1 - k, i + (ADA_UNITS // 2 + 1 + k))

                run_loop(dve, 0, FT // 2 - 1, lambda i: [tile(i, k, 2048) for k in range(2)], own,
                         2 * (2 + 2 * KC - 1) if full else 2)
                for k in range(2):
                    tile(FT // 2 - 1, k, 1024, full and k == 0)

            def feed_down(layer, after):
                name = f"down{layer}"
                cols = ROWS if layer == 0 else LAT
                U0, G0 = base(name, "w"), base(name, "g")
                H = FT // 2

                def g_split(n, chunk_, s):
                    dve.wait_ge(g_hi, n + (G0 + 1))
                    minus_hi(act_lo[:, 2 * s:2 * s + 2, 0:cols], G[:, ds(chunk_, 2), 0:cols],
                             act_hi[:, 2 * s:2 * s + 2, 0:cols], g_lo)

                for n in range(2):
                    g_split(n, 2 * n, n)

                def step(i, k, c, half, w=1024, g=True):
                    n = c + k
                    if w:
                        split_lo(i * 2 + (U0 + n + 2), n % 2, w)
                    if g:
                        g_split(i * 2 + (n + 2), i * 4 + 2 * ((n + 2) % H if half is None else n + 2 - half * H),
                                n % 2)
                for i in (0, 2):
                    run_loop(dve, i, i + 2, lambda i: [step(i, k, 0, 0) for k in range(2)])
                    if layer == 0:
                        g = FT + i // 2
                        ada_evac(ada_round(1, g - 1), (g - 1) % 2, (g - 1) // 2 + ADA_UNITS // 2 + 1)
                        ada_multiply(g % 2, g // 2 + ADA_UNITS // 2 + 1)
                step(0, 0, 8, 0)
                step(0, 0, 9, None)
                step(0, 0, 10, None)
                if layer == 0:
                    ada_evac(ada_round(1, FT + 1), 1, ADA_UNITS)
                run_loop(dve, 0, 4, lambda i: [step(i, k, 11, 1) for k in range(2)])
                step(0, 0, 19, 1)
                if after:
                    split_lo(U0 + FT, 0, after)
                modulation(("norm2", "norm4")[layer])

            own.inc(V.memset(stream[:, :, :], 0.0))
            own.wait()
            for v in range(2):
                own.inc(V.memset(stream[:, v, v:v + 1], 1.0))
            own.wait()
            V.memset(mhalf[:, :], -0.5).then_inc(o_lo, 1)
            dve.wait_ge(c_in, 16)
            dve.wait_ge(act_self, 1)
            own.inc(V.tensor_scalar_add(cexp[:, :, :], cexp[:, :, :], 1.0))
            own.wait()
            own.inc(V.reciprocal(cexp[:, :, :], cexp[:, :, :]))
            own.wait()
            V.tensor_mul(silu[:, :, :], cvec[:, :, :], cexp[:, :, :]).then_inc(sc_ready, 1)
            for g in range(ADA_FIRST):
                ada_evac(g, g % 2, g // 2 + 1)
            for u in range(2):
                split_lo(u, u, 4 * MLA_IN)
            dve.wait_ge(const_in, CONST_IN)
            own.inc(V.tensor_scalar(sinks8[:, :], sinks[:, :], 1.0 / SWA.scale, None, ALU.mult))
            modulation("norm0")
            norm("norm0")
            in_projection(0)
            attention("mla", MLA)
            attention("swa", SWA)
            out_projection(0)
            norm("norm1", lambda: split_lo(base("up0", "w") + 1, 1, 2048))
            feed_up(0)
            feed_down(0, 2048)
            norm("norm2", lambda: split_lo(base("in1", "w") + 1, 1, 2048))
            in_projection(1)
            attention("na", NA)
            attention("gqa", GQA)
            out_projection(1)
            norm("norm3", lambda: split_lo(base("up1", "w") + 1, 1, 2048))
            feed_up(1)
            feed_down(1, None)
            norm("norm4")

        @block.gpsimd
        def _(pool):
            Q = nc.gpsimd
            own = Chain(pool, pool_self)

            def ada_store(layer, r, slot, g):
                pool.wait_ge(t_free, r + 1)
                pool.dma_start(mods[layer, :, ds(g * ADA_COLS, ADA_COLS)], ada_row[:, slot, :])\
                    .then_inc(ada_out[slot], 16)

            def root(dst, src, n, sem_):
                own.inc(Q.tensor_scalar(dst, src, 1.0 / n, EPS, ALU.mult, ALU.add))
                own.wait()
                ins = Q.tensor_tensor(dst, dst, mhalf[:, 0:dst.shape[1]], ALU.pow)
                if sem_ is None:
                    own.inc(ins)
                    own.wait()
                else:
                    ins.then_inc(sem_, 1)

            def norm(name):
                y, h = NORMS[name][0] is not None, NORMS[name][1] is not None
                T, Y0, H0 = NORM_TILES[name], base(name, "y"), base(name, "h")
                xl, st = base(name, "xl"), base(name, "xs")
                for t in range(T + 1):
                    if y and t < T:
                        pool.wait_ge(sum_y, Y0 + t + 1)
                        root(rsy[:, t:t + 1], ssy[:, t:t + 1], D, rs_y)
                    if h and t:
                        q = t - 1
                        pool.wait_ge(sum_x, H0 + q + 1)
                        root(rsx[:, q:q + 1], ssx[:, q:q + 1], D, rs_x)
                    if y and t < T:
                        pool.wait_ge(y_scaled, Y0 + t + 1)
                        pool.wait_ge(x_ld[t % 2], 16 * (xl // 2 + t // 2 + 1))
                        if t >= 2 and h:
                            pool.wait_ge(h_scaled, H0 + t - 1)
                        at_least(pool, x_st[t % 2], 16 * (st // 2 + t // 2))
                        Q.tensor_add(x_new[t % 2], x_in[t % 2], Y[:, t, :]).then_inc(x_added, 1)

            def in_projection(layer):
                name = f"in{layer}"
                done, q, nsq = [base_staged[layer]], [base(name, "st")], [base(name, "nsq")]

                def stores(tiles, n, norm_widths, dst, latent=False):
                    tiles = list(tiles)

                    def rs():
                        p = nsq[0] % 2
                        nsq[0] += 1
                        pool.wait_ge(squares, nsq[0])
                        at = 0
                        for k, (w, cnt) in enumerate(norm_widths):
                            last = k == len(norm_widths) - 1
                            root(rsh[:, p, at:at + cnt], ssh[:, p, at:at + cnt], w, head_rs if last else None)
                            at += cnt

                    def store(t):
                        done[0] += 1
                        pool.wait_ge(staged, done[0])
                        if latent:
                            pool.dma_start(proj[0][t * P:(t + 1) * P, Q_RANK + KV_RANK:MLA_IN],
                                           mla_in[t][:, Q_RANK + KV_RANK:MLA_IN]).then_inc(kpe_out, 16)
                        else:
                            s = q[0] % 4
                            q[0] += 1
                            pool.dma_start(dst[0][t * P:(t + 1) * P, dst[1]:dst[1] + n], stage[s][:, 0:n])\
                                .then_inc(stage_out[s], 16)
                    for x, t in enumerate(tiles):
                        if norm_widths:
                            rs()
                            if x:
                                store(tiles[x - 1])
                        else:
                            store(t)
                    if norm_widths:
                        store(tiles[-1])

                def ada(n):
                    if layer == 0:
                        for k in range(2):
                            g = ADA_FIRST + 2 * n + k
                            ada_store(0, ada_round(0, g), k, g)
                n = 0
                widths = [[(Q_RANK, 1), (KV_RANK, 1)], [], []] if layer == 0 else [[], [], [], [(P, 4)], [(P, 2)]]
                for (c, cn, tiles), nw in zip(IN_CHUNKS[layer], widths):
                    ada(n)
                    stores(tiles, cn, nw, (proj[layer], c), latent=layer == 0 and n == 0)
                    ada(n + 1)
                    n += 2
                if layer == 0:
                    for dst, cols in ((mla_q, 384), (mla_kv, 512)):
                        for half in range(2):
                            stores(range(NT), cols, [], (dst, half * cols))
                        ada(n)
                        n += 1

            def attention(name, a):
                S0, H0 = base(name, "s"), base(name, "hd")

                def values(h, s, loaded, used):
                    wait_apart(pool, (head_in[s], loaded), (pv_done, used))
                    v = v_raw[s][:, 0:NT * a.dv].rearrange("p (t c) -> p t c", c=a.dv)
                    hi, lo = (x[:, :, 0:a.dv] for x in vs[s])
                    own.inc(Q.tensor_copy(hi, v))
                    own.wait()
                    Q.tensor_sub(lo, v, hi.bitcast(fp32)).then_inc(v_split, 1)

                def mask(s, loaded):
                    wait_apart(pool, (head_in[s], loaded))
                    b = na_bias[s].rearrange("p (r c) -> p r c", c=GRID_W)
                    Q.tensor_add(b, b, colmask[:, :].unsqueeze(1).to_broadcast([P, NA_ROWS, GRID_W]))\
                        .then_inc(bias_ready, 1)

                def scale(j, unit):
                    n, p = a.units[j][2], j % 2
                    wait_apart(pool, (rc_done, unit + 1))
                    for lo_, hi_ in ([(0, ROWS)] if n == LT else [(0, n * P), (LAT, ROWS)] if n else [(LAT, ROWS)]):
                        v = prob[p][:, lo_:hi_]
                        last = Q.tensor_scalar(v, v, rinv[:, p:p + 1], 1.0, ALU.mult, ALU.mult)
                    last.then_inc(p_scaled, 1)

                def step(i, s, j, last_pair):
                    h = i * 2 + s
                    last_head = last_pair and s == 1
                    unit = h * a.nu + (S0 + j)
                    if not (last_head and j + 2 >= a.nu):
                        scale((j + 2) % a.nu, unit + 2)
                    fills = head_fills[name][1 - s]
                    loaded = i * a.load_inc + (fills + (1 if s == 0 else 2) * a.load_inc)
                    if j == 0 and a.bias == "na" and not last_head:
                        mask(1 - s, loaded)
                    if j == a.nu - 2 and not last_head:
                        values(h + 1, 1 - s, loaded, h * a.nu + (S0 + PV0))

                if a.bias == "na":
                    mask(0, head_fills[name][0] + a.load_inc)
                values(0, 0, head_fills[name][0] + a.load_inc, S0 + PV0)
                for j in range(2):
                    scale(j, S0 + j)
                step(0, 0, 0, False)

                def body(i):
                    for s in range(2):
                        for j in range(a.nu):
                            if s or j:
                                step(i, s, j, False)
                    step(i + 1, 0, 0, False)
                run_loop(pool, 0, a.pairs - 1, body, own, 2)
                i = a.pairs - 1
                for s in range(2):
                    for j in range(a.nu):
                        if s or j:
                            step(i, s, j, True)

            pool.wait_ge(o_lo, 1)
            for g in range(ADA_FIRST):
                ada_store(0, g, g % 2, g)
            norm("norm0")

            own.inc(Q.memset(rpb[:, :], 0.0))
            own.wait()
            pool.dma_start(rpb[:, 48:48 + 31], I["na_rpb"][0].rearrange("h r c -> (h r) c")).then_inc(tz_in, 16)
            pool.wait_ge(tz_in, 16)
            own.inc(Q.tensor_scalar(rpb[:, :], rpb[:, :], 1.0 / NA.scale, 1.0, ALU.mult, ALU.mult))
            own.wait()
            pool.dma_start(toeplitz[:, :].rearrange("r (c x) -> r c x", x=TZ_W),
                           rpb[:, 0:TZ_W].unsqueeze(1).to_broadcast([8 * 15, GRID_W, TZ_W])).then_inc(tz_out, 16)
            in_projection(0)
            attention("mla", MLA)
            attention("swa", SWA)
            norm("norm1")
            T0 = base("up0", "t")
            for g in range(2):
                ada_store(1, T0 + g, g, g)
            run_loop(pool, 0, FT // 2, lambda i: [ada_store(1, i * 2 + (T0 + 2 + k), k, i * 2 + (2 + k))
                                                  for k in range(2)])
            norm("norm2")
            in_projection(1)
            attention("na", NA)
            attention("gqa", GQA)
            norm("norm3")
            norm("norm4")
            for s in range(2):
                pool.wait_ge(x_st[s], 16 * total["xs"] // 2)
                pool.wait_ge(ada_out[s], 16 * ADA_UNITS)


_INS = ["x", "ctx", "ada_w", "ada_b", "pre_mix_g", "post_mix_g", "pre_ffn_g", "post_ffn_g",
        "ffn_up", "ffn_down", "even_w_in", "even_w_out", "mla_q_norm_g",
        "mla_w_uq", "mla_kv_norm_g", "mla_w_ukv", "swa_sink", "odd_w_in", "odd_w_out", "na_rpb",
        "gqa_q_g", "gqa_k_g"]


def shape_constants():
    f32 = np.float32
    tables = {"ident": np.eye(P, dtype=f32)}
    pos = np.arange(LAT)
    for w in (16, 32, 64):
        d = 2 * w
        freqs = f32(10000.0) ** (-np.arange(d // 4, dtype=f32) * f32(4.0) / f32(d))
        rows, cols = (pos // GRID_W).astype(f32), (pos % GRID_W).astype(f32)
        ang = np.concatenate([rows[:, None] * freqs, cols[:, None] * freqs], axis=-1).astype(f32)
        t = np.stack([np.cos(ang), np.sin(ang)], axis=1)
        tables[f"rope{w}"] = np.ascontiguousarray(t.reshape(LT, P, 2, w).transpose(1, 0, 2, 3)).astype(f32)
    q, k = np.arange(P)[:, None], np.arange(P)[None, :]
    zero, neg = f32(0), f32(NEG)
    tables["band"] = np.concatenate([np.where(k >= q, zero, neg), np.zeros((P, P), f32),
                                     np.where(k <= q, zero, neg)], axis=1).astype(f32)
    c = np.arange(P)[:, None] % GRID_W
    start = np.clip(c - 8, 0, GRID_W - 16)
    kc = np.arange(GRID_W)[None, :]
    tables["colmask"] = np.where((kc >= start) & (kc < start + 16), zero, neg).astype(f32)
    return tables


def kernel(**inputs):
    import concourse.bacc as _bacc
    from concourse.bass_utils import run_bass_kernel_spmd as _run

    nc = _bacc.Bacc("TRN2", target_bir_lowering=False, num_devices=1)
    arrays, I, C = {}, {}, {}
    packed = shape_constants()
    packed["streams"] = np.stack([inputs["c"][0], inputs["c_ctx"]]).reshape(2, KC, P).transpose(2, 1, 0)
    packed["conv"] = np.concatenate([inputs["ffn_conv_w"], inputs["ffn_conv_b"][:, None]], axis=1)\
        .reshape(2, 4, FT, P).transpose(3, 0, 2, 1)
    for group, named in ((I, {n: inputs[n] for n in _INS}), (C, packed)):
        for name, a in named.items():
            a = np.ascontiguousarray(a)
            arrays[f"in_{name}"] = a
            group[name] = nc.dram_tensor(f"in_{name}", a.shape, mybir.dt.from_np(a.dtype),
                                         kind="ExternalInput").ap()
    out = nc.dram_tensor("out_0", (1, LAT, D), mybir.dt.float32, kind="ExternalOutput").ap()
    build(nc, I, C, out)
    r = _run(nc, [arrays], core_ids=[0])
    return r.results[0]["out_0"]
```
